# Optimizing a Trainium2 kernel written in Bass

```python
import math
import jax, jax.numpy as jnp
from jax import lax
import numpy as np

D_MODEL = 1024
BATCH = 1
SEQ = 512
DEPTH = 2

M_HEADS = 4
M_HEAD_DIM = 128
M_WIDTH = M_HEADS * M_HEAD_DIM
M_CONV = 4
M_CHUNK = 128
M_INIT = -1e30
ROPE_DIM = 64
ROPE_THETA = 10000.0
S_HEADS = 8
S_HEAD_DIM = ROPE_DIM
S_WIDTH = S_HEADS * S_HEAD_DIM
S_KV_RANK = 256
IDX_HEADS = 4
IDX_DIM = ROPE_DIM
IDX_TOPK_MAX = 256
S_QBLOCK = 64
DA_HEADS = 4
DA_HEAD_DIM = ROPE_DIM
DA_V_DIM = 2 * DA_HEAD_DIM
DA_WIDTH = DA_HEADS * DA_V_DIM
DA_QBLOCK = 128
N_BRANCH = 3
BRANCH_WIDTH = 512
FF_DIM = ((8 * D_MODEL + 3 * 256 - 1) // (3 * 256)) * 256
EPS = 1e-6

_SEG_SIZES = (
    2 * M_WIDTH,
    M_WIDTH,
    M_WIDTH,
    2 * M_HEADS,
    S_WIDTH,
    S_KV_RANK,
    IDX_HEADS * IDX_DIM,
    IDX_DIM,
    IDX_HEADS,
    2 * DA_HEADS * DA_HEAD_DIM,
    2 * DA_HEADS * DA_HEAD_DIM,
    DA_WIDTH,
    N_BRANCH * D_MODEL,
)
IN_COLS = sum(_SEG_SIZES)


def _split_cols(z):
    offs = []
    acc = 0
    for s in _SEG_SIZES[:-1]:
        acc += s
        offs.append(acc)
    return jnp.split(z, offs, axis=-1)

def _rms(x, g):
    xf = x.astype(jnp.float32)
    y = xf * lax.rsqrt(jnp.mean(xf * xf, axis=-1, keepdims=True) + EPS)
    return (y * g.astype(jnp.float32)).astype(x.dtype)

def _rope_tables(seq, dim, dtype):
    inv = 1.0 / jnp.power(ROPE_THETA, jnp.arange(0, dim, 2, dtype=jnp.float32) / dim)
    ang = jnp.arange(seq, dtype=jnp.float32)[:, None] * inv[None, :]
    return jnp.cos(ang).astype(dtype), jnp.sin(ang).astype(dtype)

def _rope(x, cos, sin):
    half = x.shape[-1] // 2
    shape = (1, cos.shape[0]) + (1,) * (x.ndim - 3) + (half,)
    c = cos.reshape(shape)
    s = sin.reshape(shape)
    x1, x2 = x[..., :half], x[..., half:]
    return jnp.concatenate([x1 * c - x2 * s, x1 * s + x2 * c], axis=-1)

def _causal_conv(x, w, b):
    k, c = w.shape
    y = lax.conv_general_dilated(x, w[:, None, :], window_strides=(1,), padding=[(k - 1, 0)],
                                 dimension_numbers=('NWC', 'WIO', 'NWC'), feature_group_count=c)
    return y + b

def _mlstm(q, k, v, i_pre, f_pre):
    B, T, H, dh = q.shape
    L = M_CHUNK
    N = T // L
    f32 = jnp.float32

    def chunk(a):
        a = a.astype(f32).reshape((B, N, L, H) + a.shape[3:])
        return jnp.moveaxis(a, 3, 1)

    qc = chunk(q)
    kc = chunk(k) * (dh ** -0.5)
    vc = chunk(v)
    ic = chunk(i_pre)
    lf = jax.nn.log_sigmoid(chunk(f_pre))
    b = jnp.cumsum(lf, axis=-1)
    g = b[..., -1]

    a = g[..., None] - b + ic
    m_loc = a.max(axis=-1)
    w_loc = jnp.exp(a - m_loc[..., None])
    c_loc = jnp.einsum('bhnlv,bhnlk->bhnvk', vc * w_loc[..., None], kc)
    n_loc = jnp.einsum('bhnl,bhnlk->bhnk', w_loc, kc)

    def step(state, xs):
        c_st, n_st, m_st = state
        g_n, c_n, nn_n, m_n = xs
        m_new = jnp.maximum(g_n + m_st, m_n)
        s_old = jnp.exp(g_n + m_st - m_new)
        s_loc = jnp.exp(m_n - m_new)
        c_new = s_old[..., None, None] * c_st + s_loc[..., None, None] * c_n
        n_new = s_old[..., None] * n_st + s_loc[..., None] * nn_n
        return (c_new, n_new, m_new), (c_st, n_st, m_st)

    init = (jnp.zeros((B, H, dh, dh), f32), jnp.zeros((B, H, dh), f32), jnp.full((B, H), M_INIT, f32))
    xs = (jnp.moveaxis(g, 2, 0), jnp.moveaxis(c_loc, 2, 0), jnp.moveaxis(n_loc, 2, 0), jnp.moveaxis(m_loc, 2, 0))
    _, (c_prev, n_prev, m_prev) = lax.scan(step, init, xs)
    c_prev = jnp.moveaxis(c_prev, 0, 2)
    n_prev = jnp.moveaxis(n_prev, 0, 2)
    m_prev = jnp.moveaxis(m_prev, 0, 2)

    t_idx = jnp.arange(L)
    causal = t_idx[:, None] >= t_idx[None, :]
    dmat = b[..., :, None] - b[..., None, :] + ic[..., None, :]
    dmat = jnp.where(causal, dmat, -jnp.inf)
    inter = b + m_prev[..., None]
    m_t = jnp.maximum(inter, dmat.max(axis=-1))
    sw = jnp.exp(dmat - m_t[..., None]) * jnp.einsum('bhntk,bhnsk->bhnts', qc, kc)
    s_inter = jnp.exp(inter - m_t)
    num = jnp.einsum('bhnts,bhnsv->bhntv', sw, vc) + s_inter[..., None] * jnp.einsum('bhntk,bhnvk->bhntv', qc, c_prev)
    den = sw.sum(axis=-1) + s_inter * jnp.einsum('bhntk,bhnk->bhnt', qc, n_prev)
    h = num / jnp.maximum(jnp.abs(den), jnp.exp(-m_t))[..., None]
    return jnp.moveaxis(h, 1, 3).reshape(B, T, H, dh)

def _dsa(q, k, v, qi, ki, wi):
    B, T, H, dh = q.shape
    topk = min(IDX_TOPK_MAX, T // 4)
    nb = T // S_QBLOCK
    f32 = jnp.float32
    bidx = jnp.arange(B)[:, None, None]
    ki32 = ki.astype(f32)
    key_pos = jnp.arange(T)
    idx_scale = (IDX_HEADS * IDX_DIM) ** -0.5

    def blocks(a):
        return jnp.moveaxis(a.reshape((B, nb, S_QBLOCK) + a.shape[2:]), 1, 0)

    def blk(args):
        qb, qib, wib, start = args
        tq = start + jnp.arange(S_QBLOCK)
        causal = key_pos[None, :] <= tq[:, None]
        rel = jax.nn.relu(jnp.einsum('bqhd,bsd->bqhs', qib.astype(f32), ki32))
        score = jnp.einsum('bqh,bqhs->bqs', wib.astype(f32) * idx_scale, rel)
        score = jnp.where(causal[None], score, -jnp.inf)
        _, idx = lax.top_k(score, topk)
        valid = idx <= tq[None, :, None]
        k_sel = k[bidx, idx]
        v_sel = v[bidx, idx]
        s = jnp.einsum('bqhd,bqkhd->bhqk', qb, k_sel).astype(f32) * (dh ** -0.5)
        s = jnp.where(valid[:, None], s, -jnp.inf)
        p = jax.nn.softmax(s, axis=-1).astype(v.dtype)
        return jnp.einsum('bhqk,bqkhd->bqhd', p, v_sel)

    starts = jnp.arange(nb, dtype=jnp.int32) * S_QBLOCK
    out = lax.map(blk, (blocks(q), blocks(qi), blocks(wi), starts))
    return jnp.moveaxis(out, 0, 1).reshape(B, T, H, dh)

def _diff_attn(q, k, v, lam):
    B, T, H, _, d = q.shape
    nb = T // DA_QBLOCK
    f32 = jnp.float32
    key_pos = jnp.arange(T)

    def blk(args):
        qb, start = args
        tq = start + jnp.arange(DA_QBLOCK)
        causal = key_pos[None, :] <= tq[:, None]
        s = jnp.einsum('bqhcd,bshcd->bhcqs', qb, k).astype(f32) * (d ** -0.5)
        s = jnp.where(causal, s, -jnp.inf)
        p = jax.nn.softmax(s, axis=-1)
        a = p[:, :, 0] - lam * p[:, :, 1]
        return jnp.einsum('bhqs,bshv->bqhv', a.astype(v.dtype), v)

    qblk = jnp.moveaxis(q.reshape((B, nb, DA_QBLOCK) + q.shape[2:]), 1, 0)
    starts = jnp.arange(nb, dtype=jnp.int32) * DA_QBLOCK
    out = lax.map(blk, (qblk, starts))
    return jnp.moveaxis(out, 0, 1).reshape(B, T, H, v.shape[-1])

def _layer(x, li, cos, sin, norm_mix_g, w_in, b_gate, conv_w, conv_b, gate_b, m_norm_g,
           kv_norm_g, w_kv_up, sq_g, sk_g, dq_g, dk_g, lam, d_out_g, w_branch, w_out,
           norm_ffn_g, w_gate_up, w_down):
    B, T, _ = x.shape
    f32 = jnp.float32
    xn = _rms(x, norm_mix_g)
    z = jnp.einsum('btd,dc->btc', xn, w_in)
    (m_qk, m_v, m_o, m_if, s_q, s_ckv, i_q, i_k, i_w, d_q, d_k, d_v, g_pre) = _split_cols(z)

    m_qk = jax.nn.silu(_causal_conv(m_qk, conv_w, conv_b))
    mq, mk = jnp.split(m_qk, 2, axis=-1)
    m_if = m_if + gate_b
    h = _mlstm(mq.reshape(B, T, M_HEADS, M_HEAD_DIM), mk.reshape(B, T, M_HEADS, M_HEAD_DIM),
               m_v.reshape(B, T, M_HEADS, M_HEAD_DIM), m_if[..., :M_HEADS], m_if[..., M_HEADS:])
    h = _rms(h, m_norm_g).reshape(B, T, M_WIDTH)
    y_a = (jax.nn.sigmoid(m_o.astype(f32)) * h).astype(x.dtype)

    sq = _rope(_rms(s_q.reshape(B, T, S_HEADS, S_HEAD_DIM), sq_g), cos, sin)
    ckv = _rms(s_ckv, kv_norm_g)
    kv = jnp.einsum('btr,rc->btc', ckv, w_kv_up).reshape(B, T, 2, S_HEADS, S_HEAD_DIM)
    sk = _rope(_rms(kv[:, :, 0], sk_g), cos, sin)
    sv = kv[:, :, 1]
    iq = _rope(i_q.reshape(B, T, IDX_HEADS, IDX_DIM), cos, sin)
    ik = _rope(i_k, cos, sin)
    y_b = _dsa(sq, sk, sv, iq, ik, i_w).reshape(B, T, S_WIDTH)

    dq = _rope(_rms(d_q.reshape(B, T, DA_HEADS, 2, DA_HEAD_DIM), dq_g), cos, sin)
    dk = _rope(_rms(d_k.reshape(B, T, DA_HEADS, 2, DA_HEAD_DIM), dk_g), cos, sin)
    dv = d_v.reshape(B, T, DA_HEADS, DA_V_DIM)
    lamf = lam.astype(f32)
    lam_init = 0.8 - 0.6 * math.exp(-0.3 * li)
    lam_val = jnp.exp(jnp.sum(lamf[0] * lamf[1])) - jnp.exp(jnp.sum(lamf[2] * lamf[3])) + lam_init
    o = _diff_attn(dq, dk, dv, lam_val)
    y_c = (_rms(o, d_out_g) * (1.0 - lam_init)).reshape(B, T, DA_WIDTH)

    gates = jax.nn.sigmoid((g_pre + b_gate).astype(f32)).astype(x.dtype).reshape(B, T, N_BRANCH, D_MODEL)
    merged = (gates[:, :, 0] * jnp.einsum('btc,cd->btd', y_a, w_branch[0])
              + gates[:, :, 1] * jnp.einsum('btc,cd->btd', y_b, w_branch[1])
              + gates[:, :, 2] * jnp.einsum('btc,cd->btd', y_c, w_branch[2]))
    x = x + jnp.einsum('btd,de->bte', merged, w_out)

    xn = _rms(x, norm_ffn_g)
    gu = jnp.einsum('btd,df->btf', xn, w_gate_up)
    g, u = jnp.split(gu, 2, axis=-1)
    return x + jnp.einsum('btf,fd->btd', jax.nn.silu(g) * u, w_down)

def first_inputs(seed: int = 0) -> dict:
    key = jax.random.key(seed)
    ks = jax.random.split(key, 24)
    nrm = jax.random.normal
    f32 = jnp.float32

    def gain(k, shape):
        return 1.0 + 0.02 * nrm(k, shape, f32)

    i_bias = 0.1 * nrm(ks[6], (DEPTH, M_HEADS), f32)
    f_bias = jnp.linspace(3.0, 6.0, M_HEADS, dtype=f32)[None, :] + 0.1 * nrm(ks[7], (DEPTH, M_HEADS), f32)
    return {
        'x': nrm(ks[0], (BATCH, SEQ, D_MODEL), f32),
        'norm_mix_g': gain(ks[1], (DEPTH, D_MODEL)),
        'w_in': nrm(ks[2], (DEPTH, D_MODEL, IN_COLS), f32) * D_MODEL ** -0.5,
        'b_gate': 0.02 * nrm(ks[3], (DEPTH, N_BRANCH * D_MODEL), f32),
        'mlstm_conv_w': nrm(ks[4], (DEPTH, M_CONV, 2 * M_WIDTH), f32) * M_CONV ** -0.5,
        'mlstm_conv_b': 0.02 * nrm(ks[5], (DEPTH, 2 * M_WIDTH), f32),
        'mlstm_gate_b': jnp.concatenate([i_bias, f_bias], axis=-1),
        'mlstm_norm_g': gain(ks[8], (DEPTH, M_HEADS, M_HEAD_DIM)),
        'dsa_kv_norm_g': gain(ks[9], (DEPTH, S_KV_RANK)),
        'dsa_w_kv_up': nrm(ks[10], (DEPTH, S_KV_RANK, 2 * S_WIDTH), f32) * S_KV_RANK ** -0.5,
        'dsa_q_norm_g': gain(ks[11], (DEPTH, S_HEAD_DIM)),
        'dsa_k_norm_g': gain(ks[12], (DEPTH, S_HEAD_DIM)),
        'diff_q_norm_g': gain(ks[13], (DEPTH, DA_HEAD_DIM)),
        'diff_k_norm_g': gain(ks[14], (DEPTH, DA_HEAD_DIM)),
        'diff_lambda': 0.1 * nrm(ks[15], (DEPTH, 4, DA_HEAD_DIM), f32),
        'diff_out_norm_g': gain(ks[16], (DEPTH, DA_V_DIM)),
        'w_branch': nrm(ks[17], (DEPTH, N_BRANCH, BRANCH_WIDTH, D_MODEL), f32) * BRANCH_WIDTH ** -0.5,
        'w_out': nrm(ks[18], (DEPTH, D_MODEL, D_MODEL), f32) * D_MODEL ** -0.5,
        'norm_ffn_g': gain(ks[19], (DEPTH, D_MODEL)),
        'w_gate_up': nrm(ks[20], (DEPTH, D_MODEL, 2 * FF_DIM), f32) * D_MODEL ** -0.5,
        'w_down': nrm(ks[21], (DEPTH, FF_DIM, D_MODEL), f32) * FF_DIM ** -0.5,
    }

def first_block(x, norm_mix_g, w_in, b_gate, mlstm_conv_w, mlstm_conv_b, mlstm_gate_b, mlstm_norm_g,
              dsa_kv_norm_g, dsa_w_kv_up, dsa_q_norm_g, dsa_k_norm_g, diff_q_norm_g, diff_k_norm_g,
              diff_lambda, diff_out_norm_g, w_branch, w_out, norm_ffn_g, w_gate_up, w_down):
    cos, sin = _rope_tables(x.shape[1], ROPE_DIM, x.dtype)
    for li in range(DEPTH):
        x = _layer(x, li, cos, sin, norm_mix_g[li], w_in[li], b_gate[li], mlstm_conv_w[li],
                   mlstm_conv_b[li], mlstm_gate_b[li], mlstm_norm_g[li], dsa_kv_norm_g[li],
                   dsa_w_kv_up[li], dsa_q_norm_g[li], dsa_k_norm_g[li], diff_q_norm_g[li],
                   diff_k_norm_g[li], diff_lambda[li], diff_out_norm_g[li], w_branch[li], w_out[li],
                   norm_ffn_g[li], w_gate_up[li], w_down[li])
    return x


EXPAND = 2
D_INNER = EXPAND * D_MODEL
NEG = -1e30

A_WIDTH = D_INNER // 2
POOL_SIZES = (2, 4, 8, 16)
A_GROUPS = len(POOL_SIZES)
A_GROUP_DIM = A_WIDTH // A_GROUPS
B_WIDTH = D_INNER - A_WIDTH
B_GROUPS = 4
B_GROUP_DIM = B_WIDTH // B_GROUPS
CHUNK = 128
EVEN_IN = 2 * A_WIDTH + 3 * B_WIDTH

DILATED = ((128, 1), (512, 4), (2048, 16))
N_DIL = len(DILATED)
HEAD_DIM = 128
C_SLOTS = 8
C_HEADS = C_SLOTS * N_DIL
C_WIDTH = C_SLOTS * HEAD_DIM
D_WIDTH = D_INNER - C_WIDTH
CONV_W = 3
ATTN_BLOCK = 128
QKV_WIDTH = 3 * C_HEADS * HEAD_DIM
ODD_IN = QKV_WIDTH + C_WIDTH + 4 * D_WIDTH

N_EVEN = (DEPTH + 1) // 2
N_ODD = DEPTH // 2


def rmsnorm(x, g):
    xf = x.astype(jnp.float32)
    y = xf * lax.rsqrt(jnp.mean(xf * xf, axis=-1, keepdims=True) + EPS)
    return (y * g.astype(jnp.float32)).astype(x.dtype)

def alibi_slopes(n):
    return jnp.asarray(2.0 ** (-8.0 * (np.arange(n) + 1) / n), dtype=jnp.float32)

def multiscale_pool(a, pool_w, pool_scale):
    Bn, S, _ = a.shape
    ag = a.reshape(Bn, S, A_GROUPS, A_GROUP_DIM).astype(jnp.float32)
    cs = jnp.pad(jnp.cumsum(ag, axis=1), ((0, 0), (1, 0), (0, 0), (0, 0)))
    t = jnp.arange(S)
    means = []
    for g, w in enumerate(POOL_SIZES):
        lo = jnp.maximum(t + 1 - w, 0)
        cnt = (t + 1 - lo).astype(jnp.float32)
        means.append((cs[:, 1:, g] - cs[:, lo, g]) / cnt[None, :, None])
    pooled = (jnp.stack(means, axis=2) - ag).astype(a.dtype)
    mixed = jnp.einsum('bsgc,gcd->bsgd', pooled, pool_w)
    return mixed.reshape(Bn, S, A_WIDTH) * pool_scale

def chunk_spatial_gate(u, v, ws, bs):
    Bn, S, _ = v.shape
    nc = S // CHUNK
    vg = v.reshape(Bn, nc, CHUNK, B_GROUPS, B_GROUP_DIM)
    causal = jnp.tril(jnp.ones((CHUNK, CHUNK), dtype=bool))
    w = jnp.where(causal[None], ws, jnp.zeros_like(ws))
    mixed = jnp.einsum('gts,bnsgc->bntgc', w, vg) + bs.T[None, None, :, :, None]
    return u * mixed.reshape(Bn, S, B_WIDTH)

def dilated_group_attention(q, k, v, window, dilation, slopes):
    Bn, S, H, Dh = q.shape
    unit = dilation * ATTN_BLOCK
    Sp = -(-S // unit) * unit
    pad = Sp - S
    L = Sp // dilation
    nb = L // ATTN_BLOCK
    span = window // dilation

    def to_sub(x):
        x = jnp.pad(x, ((0, 0), (0, pad), (0, 0), (0, 0)))
        return x.reshape(Bn, L, dilation, H, Dh).transpose(0, 2, 1, 3, 4)

    def band(x):
        x = jnp.pad(x, ((0, 0), (0, 0), (ATTN_BLOCK, 0), (0, 0), (0, 0)))
        x = x.reshape(Bn, dilation, nb + 1, ATTN_BLOCK, H, Dh)
        return jnp.concatenate([x[:, :, :-1], x[:, :, 1:]], axis=3)

    qb = to_sub(q).reshape(Bn, dilation, nb, ATTN_BLOCK, H, Dh)
    kb = band(to_sub(k))
    vb = band(to_sub(v))
    s = jnp.einsum('bdnqhe,bdnkhe->bdnhqk', qb, kb,
                   preferred_element_type=jnp.float32) * (Dh ** -0.5)
    qi = jnp.arange(ATTN_BLOCK)[:, None] + ATTN_BLOCK
    ki = jnp.arange(2 * ATTN_BLOCK)[None, :]
    steps = qi - ki
    band_ok = (steps >= 0) & (steps <= span)
    blk = jnp.arange(nb)[:, None, None]
    valid = band_ok[None] & ((blk > 0) | (ki >= ATTN_BLOCK)[None])
    dist = (steps * dilation).astype(jnp.float32)
    s = s - slopes[:, None, None] * dist
    s = jnp.where(valid[:, None], s, NEG)
    lse = jax.nn.logsumexp(s, axis=-1)
    p = jnp.exp(s - lse[..., None])
    o = jnp.einsum('bdnhqk,bdnkhe->bdnqhe', p.astype(v.dtype), vb)
    o = o.reshape(Bn, dilation, L, H, Dh).transpose(0, 2, 1, 3, 4).reshape(Bn, Sp, H, Dh)[:, :S]
    lse = lse.transpose(0, 1, 2, 4, 3).reshape(Bn, dilation, L, H)
    lse = lse.transpose(0, 2, 1, 3).reshape(Bn, Sp, H)[:, :S]
    return o, lse

def short_gated_conv(gb, gc, xt, conv_w):
    S = xt.shape[1]
    z = jnp.pad(gc * xt, ((0, 0), (CONV_W - 1, 0), (0, 0)))
    conv = conv_w[0] * z[:, 0:S]
    for j in range(1, CONV_W):
        conv = conv + conv_w[j] * z[:, j:j + S]
    return gb * conv

def even_layer(x, norm_g, w_in, pool_w, pool_scale, ws, bs, w_out):
    h = rmsnorm(x, norm_g)
    z = h @ w_in
    a, g_a, u, v, g_b = jnp.split(
        z, [A_WIDTH, 2 * A_WIDTH, 2 * A_WIDTH + B_WIDTH, 2 * A_WIDTH + 2 * B_WIDTH], axis=-1)
    y_a = multiscale_pool(a, pool_w, pool_scale) * jax.nn.silu(g_a)
    y_b = chunk_spatial_gate(u, v, ws, bs) * jax.nn.silu(g_b)
    return x + jnp.concatenate([y_a, y_b], axis=-1) @ w_out

def odd_layer(x, norm_g, w_in, conv_w, w_out):
    Bn, S, _ = x.shape
    h = rmsnorm(x, norm_g)
    z = h @ w_in
    o1 = QKV_WIDTH
    o2 = o1 + C_WIDTH
    qkv, g_c, d_b, d_c, d_x, g_d = jnp.split(
        z, [o1, o2, o2 + D_WIDTH, o2 + 2 * D_WIDTH, o2 + 3 * D_WIDTH], axis=-1)
    qkv = qkv.reshape(Bn, S, 3, N_DIL, C_SLOTS, HEAD_DIM)
    slopes = alibi_slopes(C_HEADS).reshape(N_DIL, C_SLOTS)
    outs, lses = [], []
    for gi, (window, dil) in enumerate(DILATED):
        o, l = dilated_group_attention(qkv[:, :, 0, gi], qkv[:, :, 1, gi], qkv[:, :, 2, gi],
                                       window, dil, slopes[gi])
        outs.append(o)
        lses.append(l)
    alpha = jax.nn.softmax(jnp.stack(lses, axis=0), axis=0)
    y_c = jnp.einsum('gbsh,gbshe->bshe', alpha.astype(x.dtype), jnp.stack(outs, axis=0))
    y_c = y_c.reshape(Bn, S, C_WIDTH) * jax.nn.silu(g_c)
    y_d = short_gated_conv(d_b, d_c, d_x, conv_w) * jax.nn.silu(g_d)
    return x + jnp.concatenate([y_c, y_d], axis=-1) @ w_out

def second_inputs(seed: int = 0) -> dict:
    key = jax.random.key(seed)
    ks = jax.random.split(key, 16)
    nrm = jax.random.normal
    f32 = jnp.float32
    return {
        "x": nrm(ks[0], (BATCH, SEQ, D_MODEL), f32),
        "even_norm": 1.0 + 0.05 * nrm(ks[1], (N_EVEN, D_MODEL), f32),
        "even_w_in": nrm(ks[2], (N_EVEN, D_MODEL, EVEN_IN), f32) * D_MODEL ** -0.5,
        "even_pool_w": nrm(ks[3], (N_EVEN, A_GROUPS, A_GROUP_DIM, A_GROUP_DIM), f32) * A_GROUP_DIM ** -0.5,
        "even_pool_scale": 1.0 + 0.1 * nrm(ks[4], (N_EVEN, A_WIDTH), f32),
        "even_ws": nrm(ks[5], (N_EVEN, B_GROUPS, CHUNK, CHUNK), f32) * CHUNK ** -0.5,
        "even_bs": 1.0 + 0.1 * nrm(ks[6], (N_EVEN, B_GROUPS, CHUNK), f32),
        "even_w_out": nrm(ks[7], (N_EVEN, D_INNER, D_MODEL), f32) * D_INNER ** -0.5,
        "odd_norm": 1.0 + 0.05 * nrm(ks[8], (N_ODD, D_MODEL), f32),
        "odd_w_in": nrm(ks[9], (N_ODD, D_MODEL, ODD_IN), f32) * D_MODEL ** -0.5,
        "odd_conv_w": nrm(ks[10], (N_ODD, CONV_W, D_WIDTH), f32) * CONV_W ** -0.5,
        "odd_w_out": nrm(ks[11], (N_ODD, D_INNER, D_MODEL), f32) * D_INNER ** -0.5,
        "final_norm": 1.0 + 0.05 * nrm(ks[12], (D_MODEL,), f32),
    }

def second_block(x, even_norm, even_w_in, even_pool_w, even_pool_scale, even_ws, even_bs,
              even_w_out, odd_norm, odd_w_in, odd_conv_w, odd_w_out, final_norm):
    h = x
    for layer in range(DEPTH):
        i = layer // 2
        if layer % 2 == 0:
            h = even_layer(h, even_norm[i], even_w_in[i], even_pool_w[i], even_pool_scale[i],
                           even_ws[i], even_bs[i], even_w_out[i])
        else:
            h = odd_layer(h, odd_norm[i], odd_w_in[i], odd_conv_w[i], odd_w_out[i])
    return rmsnorm(h, final_norm)


def setup_inputs(seed=0):
    out = dict(first_inputs(seed))
    for name, value in second_inputs(seed + 1).items():
        if name != "x":
            out[name + "_2"] = value
    return out


def reference(
    x, norm_mix_g, w_in, b_gate, mlstm_conv_w, mlstm_conv_b, mlstm_gate_b, mlstm_norm_g,
    dsa_kv_norm_g, dsa_w_kv_up, dsa_q_norm_g, dsa_k_norm_g, diff_q_norm_g, diff_k_norm_g,
    diff_lambda, diff_out_norm_g, w_branch, w_out, norm_ffn_g, w_gate_up, w_down, even_norm_2,
    even_w_in_2, even_pool_w_2, even_pool_scale_2, even_ws_2, even_bs_2, even_w_out_2,
    odd_norm_2, odd_w_in_2, odd_conv_w_2, odd_w_out_2, final_norm_2,
):
    x = first_block(
        x, norm_mix_g, w_in, b_gate, mlstm_conv_w, mlstm_conv_b, mlstm_gate_b, mlstm_norm_g,
        dsa_kv_norm_g, dsa_w_kv_up, dsa_q_norm_g, dsa_k_norm_g, diff_q_norm_g, diff_k_norm_g,
        diff_lambda, diff_out_norm_g, w_branch, w_out, norm_ffn_g, w_gate_up, w_down,
    )
    return second_block(
        x, even_norm_2, even_w_in_2, even_pool_w_2, even_pool_scale_2, even_ws_2, even_bs_2,
        even_w_out_2, odd_norm_2, odd_w_in_2, odd_conv_w_2, odd_w_out_2, final_norm_2,
    )


_drawn_inputs = setup_inputs


def setup_inputs(seed=0):
    import zlib

    import numpy as np

    out = dict(_drawn_inputs(seed))
    spreads = {}
    factors = {'b_gate': 6.873,
     'mlstm_conv_b': 3.14,
     'mlstm_norm_g': 5.177,
     'dsa_kv_norm_g': 8.0,
     'dsa_q_norm_g': 8.0,
     'dsa_k_norm_g': 8.0,
     'diff_q_norm_g': 4.37,
     'diff_k_norm_g': 4.245,
     'diff_lambda': 4.205,
     'diff_out_norm_g': 3.55,
     'even_norm_2': 7.877,
     'even_pool_scale_2': 8.0,
     'even_bs_2': 8.0,
     'odd_norm_2': 8.0}
    for name, (base, spread) in spreads.items():
        noise = np.random.default_rng([zlib.crc32(name.encode()), seed]).standard_normal(out[name].shape)
        drawn = base * np.exp(spread * noise) if base else spread * noise
        out[name] = __import__('jax').numpy.asarray(drawn.astype(out[name].dtype))
    for name, factor in factors.items():
        out[name] = (out[name] * factor).astype(out[name].dtype)
    return out
```

```python
import math
from contextlib import ExitStack

import numpy as np
import concourse.bass as bass
from concourse import mybir

F32 = mybir.dt.float32
F32R = mybir.dt.float32r
ALU = mybir.AluOpType
ACT = mybir.ActivationFunctionType
AX = mybir.AxisListType

P = 128
T = 512
NT = T // P
D = 1024
KD = D // P
DEPTH = 2
EPS = 1e-6
M_HEADS, M_DH = 4, 128
S_HEADS, S_DH = 8, 64
IDX_HEADS = 4
TOPK = 128
FF = 2816
KF = FF // P
DA_HEADS = 4
N_SLOT = 8
N_DIL = 3
DILATIONS = (1, 4, 16)
POOL_SIZES = (2, 4, 8, 16)
RAW_SLOTS = 4
SPLIT_SLOTS = 2
M_INIT = -1e30
MASKED = -1e30
CAUSAL_FILL = -3.0e38
TAKEN = -3.4e38
FAR = 1e33

IN_LAYER = dict(
    conv_raw=8, conv_acc=8, key_silu=4, mqk_ready=8, v_ready=4, mo_ready=4, small_ready=1, sq_raw=4,
    ckvq_raw=4, sk_raw=4, sv_ready=4, dq_raw=4, dk_raw=4, dv_ready=4, nab_ready=1, nab_exp=1,
    ln_ready=1, lf_ready=1, bg_ready=1, bg_taken=1, diag_ready=4, ub_ready=4, ub_taken=4, darg_ready=4,
    pex_ready=4, ms_ready=4, sw_ready=4, kt_ready=3, ktm_copied=3, vw_ready=3, cl_ready=3,
    state_ready=3, swt_ready=4, swt_copied=4, n2_ready=3, n2_taken=3, n1_ready=4, tot_ready=4,
    ya_tm=4, tr_ready=33, tr_copied=33, sq_normed=1, sk_normed=1, dq_normed=1, dk_normed=1,
    ckv_normed=1, ckv_low=2, iq_turned=1, ik_turned=1, idx_ready=12, relu_ready=12, idx_used=12,
    squares_summed=7, root_taken=7, att_s=64, att_max=64, att_neg=16, att_e=32, att_p=48, att_t=48,
    att_pt=48, att_o=48, att_y=8, y_tm=1, y_high=3, y_low=3, gate_ready=24, gate_used=24,
    merged_ready=8, silu_ready=22, hidden_used=22, hidden_ready=22)

LAYER_SEGMENTS = [
    ("conv", 8, [1024]), ("small", 1, [KD * 76]), ("ckvq", 4, [1024]), ("sq", 4, [1024]),
    ("mv", 4, [1024]), ("mo", 4, [1024]), ("kvup", 2, [1024]),
    ("dq", 4, [1024]), ("dk", 4, [1024]), ("dv", 4, [1024]),
    ("gates", 24, [1024, 512]), ("wout", 8, [1024]),
    ("ffn", KF, [1024, 1024]), ("down", 8, [768, 768, 640, 640]),
]
SEGMENTS = [(f"L{li}{n}", c, w) for li in range(DEPTH) for n, c, w in LAYER_SEGMENTS] + [
    ("epool", 4, [1024] * 6 + [512]), ("eug", 8, [1024, 1024]),
    ("eout", 8, [1024, 1024]),
    ("oslot", 8, [1024] * 7 + [768] * 4), ("od", 8, [1024] * 4),
    ("oout", 8, [1024, 1024]),
]


def first_chunks():
    at, out = 0, {}
    for name, items, widths in SEGMENTS:
        out[name] = at
        at += items * len(widths)
    return out


FIRST = first_chunks()
N_CHUNKS = sum(items * len(widths) for _, items, widths in SEGMENTS)

COLS = {"mix_g": 8, "conv_w": 32, "conv_b": 8, "b_gate": 24, "ffn_g": 8}
ROWS = {"gate_b": 8, "m_norm_g": 512, "kv_norm_g": 256, "sq_g": 64, "sk_g": 64, "dq_g": 64,
        "dk_g": 64, "lam": 256, "d_out_g": 128}
COLS2 = {"even_g": 8, "pool_scale": 8, "odd_g": 8, "conv_w": 24, "final_g": 8}


def offsets(table):
    at, out = 0, {}
    for name, n in table.items():
        out[name] = (at, at + n)
        at += n
    return out, at


COL_AT, N_COL = offsets(COLS)
ROW_AT, N_ROW = offsets(ROWS)
COL2_AT, N_COL2 = offsets(COLS2)

P_BASE = (0, 16)
DIL_BLOCKS = [[(0, m) for m in range(max(0, n - 1), n + 1)] + [(g, m) for g in (1, 2) for m in range(n + 1)]
              for n in range(NT)]
PT_BEFORE = [0]
for blocks_ in DIL_BLOCKS:
    PT_BEFORE.append(PT_BEFORE[-1] + -(-len(blocks_) // 4))
N_PT = PT_BEFORE[-1]
ROOTS = {"ckv": (256, 4), "sq": (S_DH, 32), "h": (M_DH, 16), "sk": (S_DH, 32), "dq": (S_DH, 32),
         "dk": (S_DH, 32), "yc": (2 * S_DH, 16)}
ROOT_NO = {name: i + 1 for i, name in enumerate(ROOTS)}


def build(nc, dram, weights, out):
    ctx = ExitStack()
    with ctx:
        sems = {}

        def S(name):
            if name not in sems:
                sems[name] = ctx.enter_context(nc.semaphore(name))
            return sems[name]

        def sb(stack, name, shape, dt=F32):
            return stack.enter_context(nc.sbuf_tensor(name, shape, dt))

        X = sb(ctx, "X", [P, KD, T])
        XNH, XNL = (sb(ctx, n, [P, KD, T], F32R) for n in ("XNH", "XNL"))
        RAW = sb(ctx, "RAW", [P, RAW_SLOTS, 1024])
        WH, WL = (sb(ctx, n, [P, SPLIT_SLOTS, 1024], F32R) for n in ("WH", "WL"))
        IDENT, ONES, TRI = (sb(ctx, n, [P, P]) for n in ("IDENT", "ONES", "TRI"))
        CAUSAL = sb(ctx, "CAUSAL", [P, T])
        COS, SIN = (sb(ctx, n, [P, NT, S_DH]) for n in ("COS", "SIN"))
        COL = sb(ctx, "COL", [P, DEPTH, N_COL])
        COL2 = sb(ctx, "COL2", [P, N_COL2])
        ROW = sb(ctx, "ROW", [P, N_ROW])
        EPS_C = sb(ctx, "EPS_C", [P, 1])
        POOL_C = sb(ctx, "POOL_C", [P, 2])
        SQ = sb(ctx, "SQ", [P, 2, T])
        RT = sb(ctx, "RT", [P, T])
        TMP = sb(ctx, "TMP", [P, 2, T])

        NORMED = (TMP[:, 0, :], TMP[:, 1, :], SQ[:, 0, :], SQ[:, 1, :])

        small = sb(ctx, "SMALLS", [P, 512])

        def overlay(*tensors, skip=0):
            with ExitStack() as stack:
                if skip:
                    sb(stack, f"pad_{tensors[0][0]}", [P, skip // 4])
                return [sb(stack, *t) for t in tensors]

        K = 1024
        YA, YB, YC, MQK, VEXT, SM, MS, TA, TB, SQT, SKT = overlay(
            ("YA", [P, 4, T]), ("YB", [P, 4, T]), ("YC", [P, 4, T]),
            ("MQK", [P, 8, T]), ("VEXT", [P, NT, 4, 129]), ("SM", [P, NT, 76]),
            ("MS", [P, 4 * K]),
            ("TA", [P, NT, T]), ("TB", [P, NT, T]), ("SQT", [P, 4, T]), ("SKT", [P, 4, T]))
        SV, IQT, IKT = X[:, 0:4, :], X[:, 4:6, :], X[:, 6, :]
        (HALL,) = overlay(("HALL", [P, NT, T]), skip=8 * K)
        CKVH, CKVL = overlay(("CKVH", [P, 2, T], F32R), ("CKVL", [P, 2, T], F32R), skip=16 * K)
        DQT, DKT, DV = overlay(("DQT", [P, 4, T]), ("DKT", [P, 4, T]), ("DV", [P, NT, T]), skip=24 * K)
        (MSK,) = overlay(("MSK", [P, 9 * P]), skip=8 * K)
        MO = SKT
        RELU = SQ
        SS = MS[:, :].rearrange("p (b j w) -> p b j w", b=2, j=4)
        at = [0]

        def part(n):
            at[0] += n
            return MS[:, at[0] - n:at[0]]

        DG, DM, SWT, KTM = (part(512) for _ in range(4))
        VW, TOT, CT = (part(516) for _ in range(3))
        at2 = [0]

        def tiny(n):
            at2[0] += n
            return small[:, at2[0] - n:at2[0]]

        IFG, NAB, LF, BG, U = tiny(32), tiny(16), tiny(16), tiny(32), tiny(16)
        MPREV, MAXU, RMAX, MX, GM, MLOC = tiny(20), tiny(16), tiny(16), tiny(16), tiny(4), tiny(4)
        ARG, AD, SSH, RSH = tiny(80), tiny(8), tiny(32), tiny(32)
        MXS, SUMS, RS_, NLR, LAM, WI = tiny(16), tiny(16), tiny(16), tiny(4), tiny(8), tiny(16)
        TOP8 = tiny(8)
        OMX = tiny(8)

        CONVIN = MS[:, 0:2 * (T + 4)].rearrange("p (b t) -> p b t", b=2)
        CONVACC = MS[:, 2 * (T + 4):2 * (T + 4) + 2 * T].rearrange("p (b t) -> p b t", b=2)
        YH, YL = overlay(("YH", [P, 12, T], F32R), ("YL", [P, 12, T], F32R), skip=32 * K)
        MH, ML = overlay(("MH", [P, 8, T], F32R), ("ML", [P, 8, T], F32R))
        SG, GACC = (SQ[:, 0, :], SQ[:, 1, :], RT[:, :]), TMP
        HH, HL, SILU, HT = overlay(("HH", [P, KF, T], F32R), ("HL", [P, KF, T], F32R),
                                   ("SILU", [P, 2, T]), ("HT", [P, 2, T]))
        EYH, EYL, EV = overlay(("EYH", [P, 16, T], F32R), ("EYL", [P, 16, T], F32R),
                               ("EV", [P, NT, 1024]))
        EA, ES, PLH = overlay(("EA", [P, 2, T]), ("ES", [P, 2, 2, T]), ("PLH", [P, 2, T], F32R),
                              skip=16 * K)
        (PLL,) = overlay(("PLL", [P, 2, T], F32R), skip=48 * K)
        GA, ET = SQ, TMP
        WS, BS, INV = overlay(("WS", [P, 4, P]), ("BS", [P, 4, P]), ("INV", [P, 4, 16]), skip=99840)
        OYH, OYL, OQK = overlay(("OYH", [P, 16, T], F32R), ("OYL", [P, 16, T], F32R), ("OQK", [P, 6, T]))
        OS, OPT = overlay(("OS", [P, 2, 10 * P]), ("OPT", [P, 10, P]), skip=16 * K)
        OV, GC, OO = overlay(("OV", [P, NT, 3, P]), ("GC", [P, 2, T]), ("OO", [P, 2, P]), skip=48 * K)
        OT = TMP
        DIST, SLOPE = overlay(("DIST", [P, 10 * P]), ("SLOPE", [P, 24]), skip=92 * K)
        ODC, OZ, OACC, OGD = overlay(
            ("ODC", [P, 2, T]), ("OZ", [P, 2, T + 2]), ("OACC", [P, 2, T]), ("OGD", [P, 2, T]),
            skip=64 * K)

        PS = [ctx.enter_context(nc.psum_tensor(f"PS{b}", [P, T], F32)) for b in range(8)]
        XSAVE = nc.dram_tensor("x_saved", (KD, P, T), F32).ap()

        def col(li, name):
            a, b = COL_AT[name]
            return COL[:, li, a:b]

        def row(name):
            a, b = ROW_AT[name]
            return ROW[:, a:b]

        def col2(name):
            a, b = COL2_AT[name]
            return COL2[:, a:b]

        def heads(ap, h):
            return ap.rearrange("p (h d) -> p h d", h=h)

        def since(eng, sem, value):
            if not isinstance(value, int) or value > 0:
                eng.wait_ge(sem, value)

        def looped(eng, n, body):
            body(0)
            with eng.Fori(1, n) as i:
                body(i)

        N_CONST = 10
        block = ctx.enter_context(nc.Block())

        def ring_program(eng, do, before=None):
            for name, items, widths in SEGMENTS:
                if before is not None:
                    before(name)
                c0, per = FIRST[name], len(widths)
                m = RAW_SLOTS // math.gcd(RAW_SLOTS, per)

                def turn(base, first_item, count, turns_done):
                    for j in range(count):
                        for q in range(per):
                            c = c0 + base * per + j * per + q
                            do(turns_done * RAW_SLOTS + c, c % RAW_SLOTS,
                               turns_done + (c // RAW_SLOTS + 1), weights[name][q][first_item + j])

                whole = items // m
                if whole > 1:
                    turn(0, 0, m, 0)
                    with eng.Fori(1, whole) as i:
                        turn(0, i * m, m, i * (m * per // RAW_SLOTS))
                    rest = whole * m
                else:
                    rest = 0
                turn(rest, rest, items - rest, 0)

        @block.sync
        def _(sp):
            for k in range(KD):
                sp.dma_start(X[:, k, :], dram["x"][k]).then_inc(S("x_loaded"), 16)
                if k == 0:
                    sp.dma_start(COL[:, :, :], dram["col"]).then_inc(S("consts"), 16)
                    sp.dma_start(ROW[:, :], dram["row"][0:1, :].to_broadcast([P, N_ROW])
                                 ).then_inc(S("rows_loaded"), 16)
            for t, name in ((COS, "cos"), (SIN, "sin")):
                sp.dma_start(t[:, :, :], dram[name]).then_inc(S("consts"), 16)
            for t, name in ((TRI, "tri"), (CAUSAL, "causal"), (COL2, "col2"), (IDENT, "ident")):
                sp.dma_start(t[:, :], dram[name]).then_inc(S("consts"), 16)

            def load(c, slot, nth, src):
                since(sp, S("weights_split"), c + 1 - RAW_SLOTS)
                sp.dma_start(RAW[:, slot, 0:src.shape[-1]], src).then_inc(S(f"raw{slot}"), 16)

            def consts_of(name):
                if name == "L1small":
                    for k in range(KD):
                        sp.wait_ge(S("x_updated"), 8 + k + 1)
                        sp.dma_start(XSAVE[k], X[:, k, :]).then_inc(S("x_saved"), 16)
                if name in ("L0wout", "L1wout"):
                    sp.wait_ge(S("y_low"), 3 * (int(name[1]) + 1))
                    if name == "L1wout":
                        sp.wait_ge(S("x_saved"), 16 * KD)
                    for k in range(KD):
                        sp.dma_start(X[:, k, :], dram["x"][k] if name == "L0wout" else XSAVE[k]
                                     ).then_inc(S("x_back"), 16)
                if name == "L0down":
                    sp.wait_ge(S("x_updated"), 8)
                    sp.dma_start(ROW[:, :], dram["row"][1:2, :].to_broadcast([P, N_ROW])
                                 ).then_inc(S("rows_loaded"), 16)
                if name == "L1down":
                    sp.wait_ge(S("x_updated"), 8 * 3)
                    sp.dma_start(WS[:, :, :], dram["ws"]).then_inc(S("even_consts"), 16)
                    sp.dma_start(BS[:, :, :].rearrange("p g t -> p (g t)"),
                                 dram["bs"].to_broadcast([P, 4 * P])).then_inc(S("even_consts"), 16)
                    sp.dma_start(INV[:, :, :].rearrange("p g t -> p (g t)"),
                                 dram["inv"].to_broadcast([P, 64])).then_inc(S("even_consts"), 16)
                if name == "eout":
                    sp.wait_ge(S("x_updated"), 8 * 4)
                    sp.dma_start(DIST[:, :], dram["dist"]).then_inc(S("odd_consts"), 16)
                    sp.dma_start(SLOPE[:, :], dram["slope"].to_broadcast([P, 24])
                                 ).then_inc(S("odd_consts"), 16)

            ring_program(sp, load, consts_of)
            for k in range(KD):
                sp.wait_ge(S("xn_ready"), 8 * 6 + k + 1)
                sp.dma_start(out[k], TMP[:, k % 2, :]).then_inc(S(f"stored{k % 2}"), 16)
            for t in range(2):
                sp.wait_ge(S(f"stored{t}"), 16 * KD // 2)

        @block.gpsimd
        def _(pool):
            nc.gpsimd.memset(ONES[:, :], 1.0)
            nc.gpsimd.memset(EPS_C[:, :], EPS).then_inc(S("ones_ready"), 1)
            nc.gpsimd.memset(POOL_C[:, :], 0.0).then_inc(S("pool_ready"), 1)
            pool.wait_ge(S("ones_ready"), 1)
            pool.wait_ge(S("pool_ready"), 1)

            def split(c, slot, nth, src):
                w, half = src.shape[-1], slot % SPLIT_SLOTS
                pool.wait_ge(S(f"raw{slot}"), nth * 16)
                since(pool, S("chunk_done"), c + 1 - SPLIT_SLOTS)
                nc.gpsimd.tensor_tensor(POOL_C[:, 1:2], POOL_C[:, 0:1], POOL_C[:, 0:1], ALU.add)
                nc.gpsimd.tensor_scalar(WH[:, half, 0:w], RAW[:, slot, 0:w], 1.0, 0.0, ALU.mult,
                                        ALU.add).then_inc(S("high_ready"), 1)
                pool.wait_ge(S("high_ready"), c + 1)
                nc.gpsimd.tensor_tensor(WL[:, half, 0:w], RAW[:, slot, 0:w],
                                        WH[:, half, 0:w].bitcast(F32), ALU.subtract
                                        ).then_inc(S("weights_split"), 1)

            ring_program(pool, split)

        @block.tensor
        def _(pe):
            release = [None] * 8

            def claim(*banks):
                for b in banks:
                    if release[b] is not None:
                        pe.wait_ge(*release[b])
                        release[b] = None

            def by_columns(bank, c, slot, kt, hi, lo, k0=0, first=True, last=True):
                for w, xs in ((WH, (hi, lo)), (WL, (hi,))):
                    pe.wait_ge(S("high_ready" if w is WH else "weights_split"), c + 1)
                    for k in range(kt):
                        for x in xs:
                            mm = nc.tensor.matmul(bank, w[:, slot, k * P:(k + 1) * P], x[:, k0 + k, :],
                                                  start=first and k == 0 and w is WH and x is hi,
                                                  stop=last and k == kt - 1 and w is WL)
                mm.then_inc(S("chunk_done"), 1)

            def first_pair(v, banks, c):
                pe.wait_ge(S("weights_split"), c + 2)
                for k in range(KD):
                    pe.wait_ge(S("xn_ready"), 8 * v + k + 1)
                    for j in range(2):
                        slot = (c + j) % 2
                        for p, (w, x) in enumerate(((WH, XNH), (WL, XNH), (WH, XNL))):
                            mm = nc.tensor.matmul(PS[banks[j]][:, :], w[:, slot, k * P:(k + 1) * P],
                                                  x[:, k, :], start=k == 0 and p == 0,
                                                  stop=k == KD - 1 and p == 2)
                        if k == KD - 1:
                            mm.then_inc(S("chunk_done"), 1)

            def by_tokens(outs, c, slot, ks, cols, hi, lo, n_k, shared=False):
                turns = [(w, n) for w in (WH, WL) for n in range(NT)]
                if shared:
                    turns.sort(key=lambda turn: turn[1])
                pe.wait_ge(S("high_ready"), c + 1)
                split_seen = False
                for w, n in turns:
                    if w is WL and not split_seen:
                        pe.wait_ge(S("weights_split"), c + 1)
                        split_seen = True
                    for j, k in enumerate(ks):
                        for x in (hi, lo) if w is WH else (hi,):
                            mm = nc.tensor.matmul(
                                outs[n], x[:, k, n * P:(n + 1) * P], w[:, slot, j * cols:(j + 1) * cols],
                                start=k == 0 and w is WH and x is hi, stop=k == n_k - 1 and w is WL)
                mm.then_inc(S("chunk_done"), 1)

            def token_group(name, banks, cols=T, k_per=2, n_k=KD, hi=XNH, lo=XNL, at=0):
                claim(*banks)
                for q in range(n_k // k_per):
                    c = FIRST[name] + at + q
                    by_tokens([PS[b][:, 0:cols] for b in banks], c, c % 2,
                              range(q * k_per, (q + 1) * k_per), cols, hi, lo, n_k)

            def norm(v):
                claim(7)
                for k in range(KD):
                    pe.wait_ge(S("norm_sq"), 8 * v + k + 1)
                    nc.tensor.matmul(PS[7][:, :], ONES[:, :], SQ[:, k % 2, :], start=k == 0,
                                     stop=k == KD - 1).then_inc(S("norm_summed"), 1)
                release[7] = (S("norm_root"), v + 1)

            def to_features(src, tiles, banks, sem, released):
                for f in range(tiles):
                    b = banks[f % len(banks)]
                    claim(b)
                    for n in range(NT):
                        mm = nc.tensor.transpose(PS[b][:, n * P:(n + 1) * P], src(n, f), IDENT[:, :])
                    mm.then_inc(sem, 1)
                    release[b] = released(f)

            def layer(li):
                def L(name, count=None):
                    return S(name) if count is None else (S(name), count + li * IN_LAYER[name])

                def seg(name):
                    return FIRST[f"L{li}{name}"]

                norm(2 * li)
                claim(0, 1)
                first_pair(2 * li, (0, 1), seg("conv"))
                for j in range(8):
                    b = j % 4
                    c = seg("conv") + j
                    if j >= 2:
                        claim(b)
                        by_columns(PS[b][:, :], c, c % 2, KD, XNH, XNL)
                    release[b] = L("conv_raw", j + 1)
                claim(4)
                c = seg("small")
                by_tokens([PS[4][:, n * 76:(n + 1) * 76] for n in range(NT)], c, c % 2, range(KD),
                          76, XNH, XNL, KD, shared=True)
                release[4] = L("small_ready", 1)
                for name, banks, sem in (("ckvq", (5, 6, 7, 0), "ckvq_raw"), ("sq", (1, 2, 3, 4), "sq_raw"),
                                         ("mv", (5, 6, 7, 0), "v_ready"), ("mo", (1, 2, 3, 4), "mo_ready")):
                    token_group(f"L{li}{name}", banks)
                    for n, b in enumerate(banks):
                        release[b] = L(sem, n + 1)
                claim(5)
                pe.wait_ge(*L("lf_ready", 1))
                nc.tensor.matmul(PS[5][:, 0:16], TRI[:, :], LF, start=True, stop=True)
                nc.tensor.matmul(PS[5][:, 16:32], ONES[:, :], LF, start=True, stop=True
                                 ).then_inc(L("bg_ready"), 1)
                release[5] = L("bg_taken", 1)

                pe.wait_ge(*L("ckv_normed", 1))
                to_features(lambda n, f: TB[:, n, f * P:(f + 1) * P], 2, (6, 7), L("tr_ready"),
                            lambda f: L("ckv_low", f + 1))
                pe.wait_ge(*L("sq_normed", 1))
                to_features(lambda n, f: TA[:, n, f * P:(f + 1) * P], 4, (0, 1, 2, 3), L("tr_ready"),
                            lambda f: L("tr_copied", f + 3))
                pe.wait_ge(*L("ckv_low", 2))
                token_group(f"L{li}kvup", (4, 5, 6, 7), k_per=2, n_k=2, hi=CKVH, lo=CKVL)
                for n, b in enumerate((4, 5, 6, 7)):
                    release[b] = L("sk_raw", n + 1)
                token_group(f"L{li}kvup", (0, 1, 2, 3), k_per=2, n_k=2, hi=CKVH, lo=CKVL, at=1)
                for n, b in enumerate((0, 1, 2, 3)):
                    release[b] = L("sv_ready", n + 1)
                pe.wait_ge(*L("iq_turned", 1))
                to_features(lambda n, f: TB[:, n, 256 + f * P:256 + (f + 1) * P], 2, (4, 5),
                            L("tr_ready"), lambda f: L("tr_copied", f + 7))
                pe.wait_ge(*L("ik_turned", 1))
                to_features(lambda n, f: TMP[:, 0, n * P:(n + 1) * P], 1, (6,), L("tr_ready"),
                            lambda f: L("tr_copied", 9))

                pe.wait_ge(*L("mqk_ready", 8))
                pe.wait_ge(*L("v_ready", NT))
                for n in range(NT):
                    tok = slice(n * P, (n + 1) * P)
                    b = 6 + n % 2
                    claim(b)
                    pe.wait_ge(*L("diag_ready", n + 1))
                    nc.tensor.matmul(PS[b][:, :], ONES[:, :], DG, start=True, stop=True
                                     ).then_inc(L("ub_ready"), 1)
                    release[b] = L("ub_taken", n + 1)
                    claim(0)
                    for h in range(M_HEADS):
                        mm = nc.tensor.matmul(PS[0][:, h * P:(h + 1) * P], MQK[:, h, tok],
                                              MQK[:, 4 + h, tok], start=True, stop=True)
                    mm.then_inc(L("ms_ready"), 1)
                    release[0] = L("sw_ready", n + 1)
                    if n < NT - 1:
                        claim(1)
                        for h in range(M_HEADS):
                            mm = nc.tensor.transpose(PS[1][:, h * P:(h + 1) * P], MQK[:, 4 + h, tok],
                                                     IDENT[:, :])
                        mm.then_inc(L("kt_ready"), 1)
                        release[1] = L("ktm_copied", n + 1)
                        claim(2, 3)
                        pe.wait_ge(*L("ktm_copied", n + 1))
                        pe.wait_ge(*L("vw_ready", n + 1))
                        for h in range(M_HEADS):
                            mm = nc.tensor.matmul(PS[2 + h // 2][:, h % 2 * 129:h % 2 * 129 + 129],
                                                  KTM[:, h * P:(h + 1) * P], VW[:, h * 129:(h + 1) * 129],
                                                  start=True, stop=True)
                        mm.then_inc(L("cl_ready"), 1)
                        release[2] = release[3] = L("state_ready", n + 1)
                    claim(4)
                    pe.wait_ge(*L("sw_ready", n + 1))
                    for h in range(M_HEADS):
                        mm = nc.tensor.transpose(PS[4][:, h * P:(h + 1) * P], DM[:, h * P:(h + 1) * P],
                                                 IDENT[:, :])
                    mm.then_inc(L("swt_ready"), 1)
                    release[4] = L("swt_copied", n + 1)
                    if n:
                        claim(1, 7 - n % 2)
                        pe.wait_ge(*L("state_ready", n))
                        for h in range(M_HEADS):
                            mm = nc.tensor.matmul(
                                PS[(1, 7 - n % 2)[h // 2]][:, h % 2 * 129:h % 2 * 129 + 129],
                                MQK[:, h, tok], CT[:, h * 129:(h + 1) * 129], start=True, stop=True)
                        mm.then_inc(L("n2_ready"), 1)
                        release[1] = release[7 - n % 2] = L("n2_taken", n)
                    banks = (5, 0)
                    claim(*banks)
                    pe.wait_ge(*L("swt_copied", n + 1))
                    for h in range(M_HEADS):
                        mm = nc.tensor.matmul(PS[banks[h // 2]][:, h % 2 * 129:h % 2 * 129 + 129],
                                              SWT[:, h * P:(h + 1) * P], VEXT[:, n, h, :],
                                              start=True, stop=True)
                    mm.then_inc(L("n1_ready"), 1)
                    release[banks[0]] = release[banks[1]] = L("tot_ready", n + 1)
                token_group(f"L{li}dq", (1, 2, 3, 4))
                for n, b in enumerate((1, 2, 3, 4)):
                    release[b] = L("dq_raw", n + 1)
                pe.wait_ge(*L("ya_tm", NT))
                to_features(lambda n, f: HALL[:, n, f * P:(f + 1) * P], 4, (0, 5, 6, 7), L("tr_ready"),
                            lambda f: L("tr_copied", f + 10))
                pe.wait_ge(*L("sk_normed", 1))
                to_features(lambda n, f: TA[:, n, f * P:(f + 1) * P], 4, (5, 6, 7, 0), L("tr_ready"),
                            lambda f: L("tr_copied", f + 14))
                token_group(f"L{li}dk", (1, 2, 3, 4))
                for n, b in enumerate((1, 2, 3, 4)):
                    release[b] = L("dk_raw", n + 1)
                pe.wait_ge(*L("tr_copied", 9))
                for n in range(1, NT):
                    w = (n + 1) * P
                    for h in range(IDX_HEADS):
                        b = (5, 6, 7, 0)[h]
                        claim(b)
                        half = slice(64 * (h % 2), 64 * (h % 2) + 64)
                        nc.tensor.matmul(PS[b][:, 0:w], IQT[half, h // 2, n * P:(n + 1) * P],
                                         IKT[half, 0:w], start=True, stop=True
                                         ).then_inc(L("idx_ready"), 1)
                        release[b] = L("relu_ready", 4 * (n - 1) + h + 1)
                token_group(f"L{li}dv", (1, 2, 3, 4))
                for n, b in enumerate((1, 2, 3, 4)):
                    release[b] = L("dv_ready", n + 1)
                pe.wait_ge(*L("dq_normed", 1))
                to_features(lambda n, f: TB[:, n, f * P:(f + 1) * P], 4, (5, 6, 7, 0), L("tr_ready"),
                            lambda f: L("tr_copied", f + 18))
                pe.wait_ge(*L("dk_normed", 1))
                to_features(lambda n, f: TA[:, n, f * P:(f + 1) * P], 4, (1, 2, 3, 4), L("tr_ready"),
                            lambda f: L("tr_copied", f + 22))
                pe.wait_ge(*L("tr_copied", 25))
                pe.wait_ge(*L("dv_ready", NT))

                for a in range(2):
                    QT, KT = ((DQT, DKT), (SQT, SKT))[a]
                    claim(0, 1, 2, 3, 4, 5, 6, 7)

                    def scores(q):
                        n = q // 2
                        w = (n + 1) * P
                        for j in range(4):
                            h = 4 * (q % 2) + j
                            half = slice(64 * (h % 2), 64 * (h % 2) + 64)
                            claim(j)
                            nc.tensor.matmul(PS[j][:, 0:w], QT[half, h // 2, n * P:(n + 1) * P],
                                             KT[half, h // 2, 0:w], start=True, stop=True
                                             ).then_inc(L("att_s"), 1)
                            release[j] = L("att_max", 32 * a + 4 * q + j + 1)

                    def values(q):
                        n = q // 2
                        per = 2 if a == 0 else 4
                        for j in range(per):
                            b = 4 + j % 2
                            src = 2 * j if a == 0 else j
                            claim(b)
                            pe.wait_ge(*L("att_p", P_BASE[a] + per * q + j + 1))
                            for m in range(n + 1):
                                mm = nc.tensor.transpose(PS[b][:, m * P:(m + 1) * P],
                                                         SS[:, q % 2, src, m * P:(m + 1) * P], IDENT[:, :])
                            mm.then_inc(L("att_t"), 1)
                            release[b] = L("att_pt", P_BASE[a] + per * q + j + 1)
                        for j in range(per):
                            o = 6 + n % 2
                            if q % 2 == 0 and j == 0:
                                claim(o)
                            d = P if a == 0 else S_DH
                            h = per * (q % 2) + j
                            V = DV if a == 0 else SV
                            pe.wait_ge(*L("att_pt", P_BASE[a] + per * q + j + 1))
                            for m in range(n + 1):
                                mm = nc.tensor.matmul(PS[o][:, h * d:(h + 1) * d],
                                                      TB[:, j, m * P:(m + 1) * P],
                                                      V[:, m, h * d:(h + 1) * d],
                                                      start=m == 0, stop=m == n)
                            mm.then_inc(L("att_o"), 1)
                        if q % 2:
                            release[o] = L("att_y", 4 * a + n + 1)

                    for q in range(9):
                        if q < 8:
                            scores(q)
                        if q:
                            values(q - 1)
                    pe.wait_ge(*(L("y_tm", 1), L("att_y", 8))[a])
                    to_features(lambda n, f: TA[:, n, f * P:(f + 1) * P], 4, (0, 1, 2, 3),
                                L("tr_ready"), lambda f: L("tr_copied", 4 * a + f + 26))

                pe.wait_ge(*L("y_low", 3))
                claim(0, 1, 2, 3, 4, 5)

                def merge(dt):
                    c = dt * 6 + seg("gates")
                    for r in range(3):
                        if isinstance(dt, int) and dt == 0:
                            pass
                        else:
                            pe.wait_ge(*L("gate_ready", dt * 3 + r - 2))
                            pe.wait_ge(*L("gate_used", dt * 3 + r - 2))
                        slot = (seg("gates")) % 2
                        by_columns(PS[2 * r][:, :], c + 2 * r, slot, KD, XNH, XNL)
                        by_columns(PS[2 * r + 1][:, :], c + 2 * r + 1, 1 - slot, 4,
                                   YH[:, 4 * r:4 * r + 4, :], YL[:, 4 * r:4 * r + 4, :])

                looped(pe, 8, merge)
                for r in range(3):
                    release[2 * r] = L("gate_ready", 24)
                    release[2 * r + 1] = L("gate_used", 24)
                pe.wait_ge(*L("merged_ready", 8))
                residual(f"L{li}wout", 2 * li, (6, 7), [(KD, 0)], MH, ML)
                norm(2 * li + 1)

                claim(0, 1, 2, 3)

                def up(i):
                    for t in range(2):
                        c = i * 4 + (seg("ffn") + 2 * t)
                        s = (seg("ffn") + 2 * t) % 2
                        if isinstance(i, int) and t == 0:
                            first_pair(2 * li + 1, (0, 1), c)
                            continue
                        if not (isinstance(i, int) and i == 0):
                            pe.wait_ge(*L("hidden_used", i * 2 + t - 1))
                        by_columns(PS[2 * t][:, :], c, s, KD, XNH, XNL)
                        by_columns(PS[2 * t + 1][:, :], c + 1, 1 - s, KD, XNH, XNL)

                looped(pe, KF // 2, up)
                for b in range(4):
                    release[b] = L("hidden_used", KF)
                pe.wait_ge(*L("hidden_ready", KF))
                residual(f"L{li}down", 2 * li + 1, (4, 5), [(6, 0), (6, 6), (5, 12), (5, 17)], HH, HL)

            def residual(name, update, banks, pieces, hi, lo):
                claim(*banks)
                per, c0 = len(pieces), FIRST[name]

                def pair(i):
                    for t in range(2):
                        since(pe, S("x_updated"), 8 * update + i * 2 + t - 1
                              if not (isinstance(i, int) and i == 0) else 0)
                        for q, (kt, k0) in enumerate(pieces):
                            by_columns(PS[banks[t]][:, :], i * (2 * per) + (c0 + t * per + q),
                                       (c0 + t * per + q) % 2, kt, hi, lo, k0=k0, first=q == 0,
                                       last=q == per - 1)

                looped(pe, 4, pair)
                release[banks[0]] = release[banks[1]] = (S("x_updated"), 8 * update + 8)

            pe.wait_ge(S("ones_ready"), 1)
            pe.wait_ge(S("consts"), 16 * 7)
            for li in range(DEPTH):
                layer(li)

            norm(4)
            for g in range(4):
                c = FIRST["epool"] + 7 * g
                if g == 0:
                    claim(0, 1)
                    first_pair(4, (0, 1), c)
                for t in range(4):
                    if g or t >= 2:
                        claim(t)
                        by_columns(PS[t][:, :], c + t, (c + t) % 2, KD, XNH, XNL)
                    release[t] = (S("e_a"), 2 * g + t + 1) if t < 2 else (S("e_ga"), 2 * g + t - 1)
                if g % 2 == 0:
                    claim(4, 5, 6, 7)
                for q in range(2):
                    k = 4 * (g % 2) + 2 * q
                    by_tokens([PS[4 + n][:, :] for n in range(NT)], c + 4 + q, (c + 4 + q) % 2,
                              range(k, k + 2), T, XNH, XNL, KD)
                if g % 2:
                    for n in range(NT):
                        release[4 + n] = (S("ev_ready"), 4 * (g // 2) + n + 1)
                pe.wait_ge(S("weights_split"), c + 7)
                pe.wait_ge(S("pooled_ready"), g + 1)
                slot = (c + 6) % 2
                for t in range(2):
                    claim(t)
                    for k in range(2):
                        for p, (w, x) in enumerate(((WH, PLH), (WL, PLH), (WH, PLL))):
                            mm = nc.tensor.matmul(
                                PS[t][:, :], w[:, slot, k * 256 + t * P:k * 256 + (t + 1) * P],
                                x[:, k, :], start=k == 0 and p == 0, stop=k == 1 and p == 2)
                    release[t] = (S("ey_ready"), 2 * g + t + 1)
                mm.then_inc(S("chunk_done"), 1)
            pe.wait_ge(S("ev_ready"), 8)
            pe.wait_ge(S("ws_masked"), 1)
            for j in range(8):
                b0 = 4 * (j % 2)
                claim(b0, b0 + 1, b0 + 2)
                for n in range(NT):
                    mm = nc.tensor.matmul(PS[b0][:, n * P:(n + 1) * P], EV[:, n, j * P:(j + 1) * P],
                                          WS[:, j // 2, :], start=True, stop=True)
                mm.then_inc(S("e_mixed"), 1)
                c = FIRST["eug"] + 2 * j
                by_columns(PS[b0 + 1][:, :], c, c % 2, KD, XNH, XNL)
                by_columns(PS[b0 + 2][:, :], c + 1, (c + 1) % 2, KD, XNH, XNL)
                release[b0] = release[b0 + 1] = release[b0 + 2] = (S("ey_ready"), 8 + j + 1)
            pe.wait_ge(S("ey_ready"), 16)
            residual("eout", 4, (3, 7), [(KD, 0), (KD, 8)], EYH, EYL)

            norm(5)
            claim(0, 1, 2, 3, 4, 5, 6, 7)

            def slot_body(i, t):
                per = 11
                c0 = FIRST["oslot"] + t * per
                first = isinstance(i, int) and i == 0 and t == 0

                def c(q):
                    return i * (2 * per) + (c0 + q), (c0 + q) % 2

                def reuse(name, per_slot, k):
                    if not first:
                        pe.wait_ge(S(name), i * (2 * per_slot) + ((t - 1) * per_slot + k))

                s = i * 2 + t
                if first:
                    first_pair(5, (0, 1), c0)
                for q in range(2 if first else 0, 6):
                    if q < 4:
                        reuse("o_sc" if q < 3 else "oy_ready", 12 if q < 3 else 1, 12 if q < 3 else 1)
                    else:
                        pe.wait_ge(S("oqk_ready"), s * 6 + (q - 3))
                    cc, sl = c(q)
                    by_columns(PS[q % 4][:, :], cc, sl, KD, XNH, XNL)
                reuse("oy_ready", 1, 1)
                cc, sl = c(6)
                by_columns(PS[6][:, :], cc, sl, KD, XNH, XNL)
                pe.wait_ge(S("oqk_ready"), s * 6 + 6)
                pe.wait_ge(S("ogc_ready"), s + 1)
                for q in range(4):
                    cc, sl = c(7 + q)
                    by_tokens([PS[(2, 3, 4, 5)[n]][:, 0:384] for n in range(NT)], cc, sl,
                              range(2 * q, 2 * q + 2), 384, XNH, XNL, KD)
                pe.wait_ge(S("ov_ready"), s * 4 + 4)
                for n in range(NT + 1):
                    if n < NT:
                        if n:
                            pe.wait_ge(S("o_sc"), s * 12 + 3 * n)
                        for g in range(N_DIL):
                            k0 = max(0, n - 1) * P if g == 0 else 0
                            nc.tensor.matmul(PS[g][:, 0:(n + 1) * P - k0], OQK[:, g, n * P:(n + 1) * P],
                                             OQK[:, 3 + g, k0:(n + 1) * P], start=True, stop=True
                                             ).then_inc(S("o_s"), 1)
                    if n:
                        m = n - 1
                        blocks = DIL_BLOCKS[m]
                        pe.wait_ge(S("o_p"), s * 4 + n)
                        for r in range(0, len(blocks), 4):
                            b = 4 + r // 4 % 2
                            if r == 8:
                                pe.wait_ge(S("o_pt"), s * N_PT + (PT_BEFORE[m] + 1))
                            for e in range(r, min(r + 4, len(blocks))):
                                mm = nc.tensor.transpose(PS[b][:, (e - r) * P:(e - r + 1) * P],
                                                         OS[:, m % 2, e * P:(e + 1) * P], IDENT[:, :])
                            mm.then_inc(S("o_t"), 1)
                        pe.wait_ge(S("o_pt"), s * N_PT + PT_BEFORE[m + 1])
                        if m >= 2:
                            pe.wait_ge(S("o_on"), s * 4 + (m - 1))
                        o = PS[6][:, (m % 2) * P:(m % 2 + 1) * P] if m % 2 == 0 else PS[7][:, 0:P]
                        for e, (g, kt) in enumerate(blocks):
                            mm = nc.tensor.matmul(o, OPT[:, e, :], OV[:, kt, g, :], start=e == 0,
                                                  stop=e == len(blocks) - 1)
                        mm.then_inc(S("o_o"), 1)
                        pe.wait_ge(S("o_on"), s * 4 + n)
                        nc.tensor.transpose(PS[3][:, m * P:(m + 1) * P], OO[:, m % 2, :], IDENT[:, :]
                                            ).then_inc(S("o_ot"), 1)

            def two_slots(i):
                slot_body(i, 0)
                slot_body(i, 1)

            looped(pe, 4, two_slots)
            pe.wait_ge(S("oy_ready"), 8)

            def conv_pair(i):
                for t in range(2):
                    for q in range(4):
                        if not (isinstance(i, int) and i == 0):
                            pe.wait_ge(S(("od_c", "od_x", "od_b", "od_g")[q]), i * 2 + t - 1)
                        by_columns(PS[4 * t + q][:, :], i * 8 + (FIRST["od"] + 4 * t + q),
                                   (FIRST["od"] + q) % 2, KD, XNH, XNL)

            looped(pe, 4, conv_pair)
            for q in range(4):
                release[q] = release[4 + q] = (S(("od_c", "od_x", "od_b", "od_g")[q]), 8)
            pe.wait_ge(S("od_ready"), 8)
            residual("oout", 5, (0, 4), [(KD, 0), (KD, 8)], OYH, OYL)
            norm(6)

        @block.scalar
        def _(act):
            def run(out_, in_, func, sem, **more):
                nc.scalar.activation(out_, in_, func, **more).then_inc(sem, 1)

            def norm(v):
                for k in range(KD):
                    if v == 0:
                        if k == 0:
                            act.wait_ge(S("x_loaded"), 16 * KD)
                    else:
                        act.wait_ge(S("x_updated"), 8 * (v - 1) + k + 1)
                    if k >= 2 or v:
                        act.wait_ge(S("norm_summed"), 8 * v + k - 1)
                    run(SQ[:, k % 2, :], X[:, k, :], ACT.Square, S("norm_sq"))
                act.wait_ge(S("norm_summed"), 8 * v + 8)
                run(RT[:, :], PS[7][:, :], ACT.Sqrt, S("norm_root"), scale=1.0 / D, bias=EPS_C[:, 0:1])
                for k in range(KD if v < 6 else 0):
                    act.wait_ge(S("xn_scaled"), 8 * v + k + 1)
                    run(XNH[:, k, :], NORMED[k % 4], ACT.Copy, S("xn_high"))

            def layer(li):
                def L(name, count=None):
                    return S(name) if count is None else (S(name), count + li * IN_LAYER[name])

                def seg(name):
                    return FIRST[f"L{li}{name}"]

                def chunk(c):
                    act.wait_ge(S("chunk_done"), c)

                def root(name):
                    length, n = ROOTS[name]
                    act.wait_ge(*L("squares_summed", ROOT_NO[name]))
                    run(RSH[:, 0:n], SSH[:, 0:n], ACT.Sqrt, L("root_taken"), scale=1.0 / length,
                        bias=EPS_C[:, 0:1])

                def take(b, dst, width, index):
                    act.wait_ge(*L("tr_ready", index))
                    run(dst, PS[b][:, 0:width], ACT.Copy, L("tr_copied"))

                norm(2 * li)
                for j in range(9):
                    if j < 8:
                        chunk(seg("conv") + j + 1)
                        if j >= 2:
                            act.wait_ge(*L("conv_acc", j - 1))
                        run(CONVIN[:, j % 2, 3:3 + T], PS[j % 4][:, :], ACT.Copy, L("conv_raw"))
                    if j:
                        q = j - 1
                        act.wait_ge(*L("conv_acc", q + 1))
                        if q < 4:
                            run(MQK[:, q, :], CONVACC[:, q % 2, :], ACT.Silu, L("mqk_ready"))
                        else:
                            run(MQK[:, q, :], CONVACC[:, q % 2, :], ACT.Silu, L("key_silu"))
                            act.wait_ge(*L("key_silu", q - 3))
                            run(MQK[:, q, :], MQK[:, q, :], ACT.Copy, L("mqk_ready"), scale=M_DH ** -0.5)
                chunk(seg("small") + 1)
                run(SM[:, :, :].rearrange("p n c -> p (n c)"), PS[4][:, 0:4 * 76], ACT.Copy,
                    L("small_ready"))
                act.wait_ge(*L("nab_ready", 1))
                run(LAM[:, 2:4], LAM[:, 0:2], ACT.Exp, L("lam_exp"))
                run(NAB, NAB, ACT.Exp, L("nab_exp"))
                act.wait_ge(*L("nab_exp", 1))
                run(NAB, NAB, ACT.Ln, L("ln_ready"), bias=ONES[:, 0:1])
                chunk(seg("ckvq") + 4)
                for n, b in enumerate((5, 6, 7, 0)):
                    run(TB[:, n, :], PS[b][:, :], ACT.Copy, L("ckvq_raw"))
                root("ckv")
                chunk(seg("sq") + 4)
                for n, b in enumerate((1, 2, 3, 4)):
                    run(TA[:, n, :], PS[b][:, :], ACT.Copy, L("sq_raw"))
                root("sq")
                chunk(seg("mv") + 4)
                for n, b in enumerate((5, 6, 7, 0)):
                    run(VEXT[:, n, :, 0:M_DH], heads(PS[b][:, :], 4), ACT.Copy, L("v_ready"))
                chunk(seg("mo") + 4)
                for n, b in enumerate((1, 2, 3, 4)):
                    run(MO[:, n, :], PS[b][:, :], ACT.Sigmoid, L("mo_ready"))
                for f in range(2):
                    take(6 + f, CKVH[:, f, :], T, f + 1)
                for f in range(4):
                    take(f, SQT[:, f, :], T, f + 3)
                if li:
                    act.wait_ge(S("x_saved"), 16 * KD)
                chunk(seg("kvup") + 1)
                for n, b in enumerate((4, 5, 6, 7)):
                    run(TA[:, n, :], PS[b][:, :], ACT.Copy, L("sk_raw"))
                chunk(seg("kvup") + 2)
                for n, b in enumerate((0, 1, 2, 3)):
                    run(SV[:, n, :], PS[b][:, :], ACT.Copy, L("sv_ready"))
                for f in range(2):
                    take(4 + f, IQT[:, f, :], T, f + 7)
                take(6, IKT[:, :], T, 9)
                for n in range(NT):
                    if n < NT - 1:
                        act.wait_ge(*L("kt_ready", n + 1))
                        if n:
                            act.wait_ge(*L("cl_ready", n))
                        run(KTM, PS[1][:, :], ACT.Copy, L("ktm_copied"))
                    act.wait_ge(*L("darg_ready", n + 1))
                    run(DM, DM, ACT.Exp, L("pex_part"))
                    run(ARG[:, 20 * n:20 * n + 20], ARG[:, 20 * n:20 * n + 20], ACT.Exp, L("pex_ready"))
                    act.wait_ge(*L("swt_ready", n + 1))
                    if n:
                        act.wait_ge(*L("n1_ready", n))
                    run(SWT, PS[4][:, :], ACT.Copy, L("swt_copied"))
                root("h")
                chunk(seg("dq") + 4)
                for n, b in enumerate((1, 2, 3, 4)):
                    run(TB[:, n, :], PS[b][:, :], ACT.Copy, L("dq_raw"))
                for f in range(4):
                    take((0, 5, 6, 7)[f], YA[:, f, :], T, f + 10)
                root("sk")
                for f in range(4):
                    take((5, 6, 7, 0)[f], SKT[:, f, :], T, f + 14)
                root("dq")
                chunk(seg("dk") + 4)
                for n, b in enumerate((1, 2, 3, 4)):
                    run(TA[:, n, :], PS[b][:, :], ACT.Copy, L("dk_raw"))
                act.wait_ge(*L("dq_normed", 1))
                for n in range(1, NT):
                    for h in range(IDX_HEADS):
                        i = 4 * (n - 1) + h
                        act.wait_ge(*L("idx_ready", i + 1))
                        if i >= 2:
                            act.wait_ge(*L("idx_used", i - 1))
                        w = (n + 1) * P
                        run(RELU[:, i % 2, 0:w], PS[(5, 6, 7, 0)[h]][:, 0:w], ACT.Relu, L("relu_ready"))
                root("dk")
                chunk(seg("dv") + 4)
                for n, b in enumerate((1, 2, 3, 4)):
                    run(DV[:, n, :], PS[b][:, :], ACT.Copy, L("dv_ready"))
                for f in range(4):
                    take((5, 6, 7, 0)[f], DQT[:, f, :], T, f + 18)
                for f in range(4):
                    take((1, 2, 3, 4)[f], DKT[:, f, :], T, f + 22)
                for a in range(2):
                    per = 2 if a == 0 else 4
                    for q in range(9):
                        if q < 8:
                            n = q // 2
                            w = (n + 1) * P
                            act.wait_ge(*L("att_neg", 8 * a + q + 1))
                            for j in range(4):
                                i = 8 * (n % 2) + 4 * (q % 2) + j
                                run(SS[:, q % 2, j, 0:w], SS[:, q % 2, j, 0:w], ACT.Exp,
                                    L("att_e") if a == 0 else L("att_p"), bias=MXS[:, i:i + 1],
                                    accum_out=SUMS[:, i:i + 1])
                        if q:
                            w = ((q - 1) // 2 + 1) * P
                            for j in range(per):
                                act.wait_ge(*L("att_t", P_BASE[a] + per * (q - 1) + j + 1))
                                run(TB[:, j, 0:w], PS[4 + j % 2][:, 0:w], ACT.Copy, L("att_pt"))
                    if a == 0:
                        root("yc")
                    for f in range(4):
                        take(f, (YC, YB)[a][:, f, :], T, 4 * a + f + 26)
                act.wait_ge(*L("tr_copied", 33))
                for i, Y in enumerate((YA, YB, YC)):
                    run(YH[:, 4 * i:4 * i + 4, :], Y[:, :, :], ACT.Copy, L("y_high"))

                def gates(dt):
                    for r in range(3):
                        act.wait_ge(S("chunk_done"), dt * 6 + (seg("gates") + 2 * r + 1))
                        if not isinstance(dt, int):
                            act.wait_ge(*L("gate_used", dt * 3 + (r - 2)))
                        act.wait_ge(S("consts"), 16 * 7)
                        run(SG[r], PS[2 * r][:, :], ACT.Sigmoid, L("gate_ready"),
                            bias=COL[:, li, bass.ds(dt + (COL_AT["b_gate"][0] + 8 * r), 1)])

                looped(act, 8, gates)
                norm(2 * li + 1)

                def silu(i):
                    for t in range(2):
                        act.wait_ge(S("chunk_done"), i * 4 + (seg("ffn") + 2 * t + 1))
                        if not isinstance(i, int):
                            act.wait_ge(*L("hidden_used", i * 2 + (t - 1)))
                        run(SILU[:, t, :], PS[2 * t][:, :], ACT.Silu, L("silu_ready"))

                looped(act, KF // 2, silu)

            act.wait_ge(S("ones_ready"), 1)
            act.wait_ge(S("consts"), 16 * 7)
            for li in range(DEPTH):
                layer(li)

            norm(4)
            for g in range(4):
                c = FIRST["epool"] + 7 * g
                for t in range(2):
                    act.wait_ge(S("chunk_done"), c + t + 1)
                    since(act, S("pooled_ready"), g)
                    run(EA[:, t, :], PS[t][:, :], ACT.Copy, S("e_a"))
                for t in range(2):
                    act.wait_ge(S("chunk_done"), c + t + 3)
                    since(act, S("ey_ready"), 2 * g)
                    run(GA[:, t, :], PS[2 + t][:, :], ACT.Silu, S("e_ga"))
                if g % 2:
                    act.wait_ge(S("chunk_done"), c + 6)
                    for n in range(NT):
                        run(EV[:, n, (g // 2) * T:(g // 2 + 1) * T], PS[4 + n][:, :], ACT.Copy,
                            S("ev_ready"))
            for j in range(8):
                act.wait_ge(S("chunk_done"), FIRST["eug"] + 2 * j + 2)
                act.wait_ge(S("ey_ready"), 8 + max(0, j - 1))
                run(GA[:, j % 2, :], PS[4 * (j % 2) + 2][:, :], ACT.Silu, S("e_gb"))

            norm(5)

            def slots(i):
                for t in range(2):
                    s = i * 2 + t
                    c0 = FIRST["oslot"] + 11 * t
                    for q in range(6):
                        act.wait_ge(S("chunk_done"), i * 22 + (c0 + q + 1))
                        run(OQK[:, q, :], PS[q % 4][:, :], ACT.Copy, S("oqk_ready"),
                            scale=P ** -0.5 if q < 3 else 1.0)
                    act.wait_ge(S("chunk_done"), i * 22 + (c0 + 7))
                    if not isinstance(i, int):
                        act.wait_ge(S("oy_ready"), i * 2 + (t - 1))
                    run(GC[:, t, :], PS[6][:, :], ACT.Silu, S("ogc_ready"))
                    act.wait_ge(S("chunk_done"), i * 22 + (c0 + 11))
                    for n in range(NT):
                        run(OV[:, n, :, :], heads(PS[2 + n][:, 0:384], 3), ACT.Copy, S("ov_ready"))
                    for n in range(NT + 1):
                        if n < NT:
                            w = len(DIL_BLOCKS[n]) * P
                            act.wait_ge(S("o_neg"), s * 4 + (n + 1))
                            run(OS[:, n % 2, 0:w], OS[:, n % 2, 0:w], ACT.Exp, S("o_p"),
                                bias=OMX[:, n:n + 1], accum_out=OMX[:, 4 + n:5 + n])
                        if n:
                            nb = len(DIL_BLOCKS[n - 1])
                            for r in range(0, nb, 4):
                                e = min(4, nb - r)
                                act.wait_ge(S("o_t"), s * N_PT + (PT_BEFORE[n - 1] + r // 4 + 1))
                                run(OPT[:, r:r + e, :], heads(PS[4 + r // 4 % 2][:, 0:e * P], e),
                                    ACT.Copy, S("o_pt"))

            looped(act, 4, slots)

            def conv_gates(i):
                for t in range(2):
                    act.wait_ge(S("chunk_done"), i * 8 + (FIRST["od"] + 4 * t + 1))
                    if not isinstance(i, int):
                        act.wait_ge(S("od_x"), i * 2 + (t - 1))
                    run(ODC[:, t, :], PS[4 * t][:, :], ACT.Copy, S("od_c"))
                    act.wait_ge(S("chunk_done"), i * 8 + (FIRST["od"] + 4 * t + 4))
                    if not isinstance(i, int):
                        act.wait_ge(S("od_ready"), i * 2 + (t - 1))
                    run(OGD[:, t, :], PS[4 * t + 3][:, :], ACT.Silu, S("od_g"))

            looped(act, 4, conv_gates)
            norm(6)

        @block.vector
        def _(dve):
            V = nc.vector
            steps = {"n": 0, "i": None, "per": 0}

            def then(ins):
                ins.then_inc(S("dve_step"), 1)
                steps["n"] += 1
                if steps["i"] is None:
                    dve.wait_ge(S("dve_step"), steps["n"])
                else:
                    dve.wait_ge(S("dve_step"), steps["i"] * steps["per"] + (steps["n"] - steps["per"]))

            def steady(n, body):
                before = steps["n"]
                body(0)
                steps["per"] = steps["n"] - before
                with dve.Fori(1, n) as i:
                    steps["i"] = i
                    body(i)
                    assert steps["n"] == before + 2 * steps["per"]
                steps["i"] = None
                steps["n"] = before + n * steps["per"]

            def norm(v, g, final=False):
                dve.wait_ge(S("norm_root"), v + 1)
                then(V.reciprocal(RT[:, :], RT[:, :]))
                for k in range(KD if final else 0):
                    if k >= 2:
                        dve.wait_ge(S(f"stored{k % 2}"), 16 * (k // 2))
                    V.scalar_tensor_tensor(TMP[:, k % 2, :], X[:, k, :], g[:, k:k + 1], RT[:, :],
                                           ALU.mult, ALU.mult).then_inc(S("xn_ready"), 1)
                for k in range(0 if final else KD + 2):
                    if k < KD:
                        if k >= 4:
                            dve.wait_ge(S("xn_ready"), 8 * v + k - 3)
                        V.scalar_tensor_tensor(NORMED[k % 4], X[:, k, :], g[:, k:k + 1], RT[:, :],
                                               ALU.mult, ALU.mult).then_inc(S("xn_scaled"), 1)
                    if k >= 2:
                        j = k - 2
                        dve.wait_ge(S("xn_high"), 8 * v + j + 1)
                        V.tensor_tensor(XNL[:, j, :], NORMED[j % 4], XNH[:, j, :].bitcast(F32),
                                        ALU.subtract).then_inc(S("xn_ready"), 1)

            def add_residual(update, banks, c0, per):
                if update in (0, 2):
                    dve.wait_ge(S("x_back"), 16 * KD * (update // 2 + 1))
                def pair(i):
                    for t in range(2):
                        dve.wait_ge(S("chunk_done"), i * (2 * per) + (c0 + (t + 1) * per))
                        x = X[:, bass.ds(i * 2 + t, 1), :].rearrange("p a t -> p (a t)")
                        V.tensor_tensor(x, x, PS[banks[t]][:, :], ALU.add
                                        ).then_inc(S("x_updated"), 1)
                looped(dve, 4, pair)

            def split(dst_hi, dst_lo, src, sem):
                then(V.tensor_scalar(dst_hi, src, 1.0, 0.0, ALU.mult, ALU.add))
                V.tensor_tensor(dst_lo, src, dst_hi.bitcast(F32), ALU.subtract).then_inc(sem, 1)

            def layer(li):
                def L(name, count=None):
                    return S(name) if count is None else (S(name), count + li * IN_LAYER[name])

                def seg(name):
                    return FIRST[f"L{li}{name}"]

                def bcast(ap, h, d):
                    return ap.unsqueeze(2).to_broadcast([P, h, d])

                def over(ap, h):
                    return ap.unsqueeze(1).to_broadcast([P, h, ap.shape[-1]])

                def ask_root(name):
                    _, n = ROOTS[name]
                    dve.wait_ge(*L("root_taken", ROOT_NO[name]))
                    then(V.reciprocal(RSH[:, 0:n], RSH[:, 0:n]))

                def squares(src, h, name):
                    for n in range(NT):
                        x = src(n)
                        sq = SQ[:, n % 2, 0:x.shape[-1]]
                        then(V.tensor_tensor(sq, x, x, ALU.mult))
                        ins = V.tensor_reduce(SSH[:, n * h:(n + 1) * h], heads(sq, h), AX.X, ALU.add)
                    ins.then_inc(L("squares_summed"), 1)
                    ask_root(name)

                def rope_tables(g):
                    half = S_DH // 2
                    COSG = TMP[:, 0, 0:256].rearrange("p (n d) -> p n d", n=NT)
                    SING = TMP[:, 0, 256:512].rearrange("p (n d) -> p n d", n=NT)
                    V.tensor_tensor(COSG, COS[:, :, :], over(g, NT), ALU.mult)
                    V.tensor_tensor(SING[:, :, 0:half], SIN[:, :, 0:half], over(g[:, half:], NT), ALU.mult)
                    then(V.tensor_tensor(SING[:, :, half:], SIN[:, :, half:], over(g[:, 0:half], NT),
                                         ALU.mult))
                    return COSG, SING

                def turn(x, h, cos, sin, dst):
                    half = S_DH // 2
                    x3, turned = heads(x, h), heads(SQ[:, 0, 0:h * S_DH], h)
                    V.tensor_tensor(turned[:, :, 0:half], x3[:, :, half:], over(sin[:, 0:half], h), ALU.mult)
                    V.tensor_tensor(turned[:, :, half:], x3[:, :, 0:half], over(sin[:, half:], h), ALU.mult)
                    straight = heads(SQ[:, 1, 0:h * S_DH], h)
                    then(V.tensor_tensor(straight, x3, over(cos, h), ALU.mult))
                    return V.tensor_tensor(dst, straight, turned, ALU.add)

                def norm_and_turn(buf, gain, name):
                    squares(lambda n: buf[:, n, :], S_HEADS, name)
                    COSG, SING = rope_tables(row(gain))
                    for n in range(NT):
                        then(V.tensor_tensor(heads(buf[:, n, :], 8), heads(buf[:, n, :], 8),
                                             bcast(RSH[:, 8 * n:8 * n + 8], 8, S_DH), ALU.mult))
                        ins = turn(buf[:, n, :], 8, COSG[:, n, :], SING[:, n, :], heads(buf[:, n, :], 8))
                        if n < NT - 1:
                            then(ins)
                    ins.then_inc(L(f"{name}_normed"), 1)
                    dve.wait_ge(*L(f"{name}_normed", 1))

                norm(2 * li, col(li, "mix_g"))
                then(V.memset(CONVIN[:, :, 0:3], 0.0))
                V.memset(VEXT[:, :, :, M_DH:M_DH + 1], 1.0)
                w, b = col(li, "conv_w"), col(li, "conv_b")
                for j in range(8):
                    acc = CONVACC[:, j % 2, :]
                    dve.wait_ge(*L("conv_raw", j + 1))
                    if j >= 2:
                        dve.wait_ge(*L("mqk_ready", j - 1))
                    then(V.tensor_scalar(acc, CONVIN[:, j % 2, 3:3 + T], w[:, 24 + j:25 + j],
                                         b[:, j:j + 1], ALU.mult, ALU.add))
                    for tap in range(3):
                        ins = V.scalar_tensor_tensor(acc, CONVIN[:, j % 2, tap:tap + T],
                                                     w[:, 8 * tap + j:8 * tap + j + 1], acc,
                                                     ALU.mult, ALU.add)
                        if tap < 2:
                            then(ins)
                    ins.then_inc(L("conv_acc"), 1)

                dve.wait_ge(S("rows_loaded"), 16 * (li + 1))
                lam = row("lam").rearrange("p (a b d) -> p a b d", a=2, b=2)
                then(V.tensor_tensor(TMP[:, 1, 0:128].rearrange("p (a d) -> p a d", a=2), lam[:, :, 0, :],
                                     lam[:, :, 1, :], ALU.mult))
                V.tensor_reduce(LAM[:, 0:2], heads(TMP[:, 1, 0:128], 2), AX.X, ALU.add)
                lam_init = 0.8 - 0.6 * math.exp(-0.3 * li)
                V.tensor_scalar(row("d_out_g"), row("d_out_g"), 1.0 - lam_init, 0.0, ALU.mult, ALU.add)
                dve.wait_ge(*L("small_ready", 1))
                ifg = IFG.rearrange("p (n c) -> p n c", n=NT)
                then(V.tensor_tensor(ifg, SM[:, :, 68:76], over(row("gate_b"), NT), ALU.add))
                i_pre, f_pre = ifg[:, :, 0:4], ifg[:, :, 4:8]
                V.scalar_tensor_tensor(NAB.rearrange("p (n c) -> p n c", n=NT), f_pre, -1.0, f_pre,
                                       ALU.mult, ALU.min).then_inc(L("nab_ready"), 1)
                V.tensor_scalar(WI.rearrange("p (n c) -> p n c", n=NT), SM[:, :, 64:68],
                                (IDX_HEADS * 64) ** -0.5, 0.0, ALU.mult, ALU.add)
                dve.wait_ge(*L("ln_ready", 1))
                V.scalar_tensor_tensor(LF.rearrange("p (n c) -> p n c", n=NT), f_pre, 0.0,
                                       NAB.rearrange("p (n c) -> p n c", n=NT), ALU.min,
                                       ALU.subtract).then_inc(L("lf_ready"), 1)
                V.scalar_tensor_tensor(LAM[:, 4:5], LAM[:, 3:4], -lam_init, LAM[:, 2:3], ALU.add,
                                       ALU.subtract)
                dve.wait_ge(*L("ckvq_raw", NT))
                squares(lambda n: TB[:, n, 0:256], 1, "ckv")
                for n in range(NT):
                    x = TB[:, n, 0:256]
                    ins = V.scalar_tensor_tensor(x, x, RSH[:, n:n + 1], row("kv_norm_g"), ALU.mult, ALU.mult)
                ins.then_inc(L("ckv_normed"), 1)
                dve.wait_ge(*L("ckv_normed", 1))
                dve.wait_ge(*L("sq_raw", NT))
                norm_and_turn(TA, "sq_g", "sq")
                for n in range(NT):
                    x = TB[:, n, 256:512]
                    ins = turn(x, 4, COS[:, n, :], SIN[:, n, :], heads(x, 4))
                    if n < NT - 1:
                        then(ins)
                ins.then_inc(L("iq_turned"), 1)
                dve.wait_ge(*L("iq_turned", 1))
                for n in range(NT):
                    x = TMP[:, 0, n * P:n * P + 64]
                    then(turn(SM[:, n, 0:64], 1, COS[:, n, :], SIN[:, n, :], heads(x, 1)))
                    ins = V.tensor_copy(TMP[:, 0, n * P + 64:(n + 1) * P], x)
                ins.then_inc(L("ik_turned"), 1)
                for f in range(2):
                    dve.wait_ge(*L("tr_copied", 1 + f))
                    V.tensor_tensor(CKVL[:, f, :], PS[6 + f][:, :], CKVH[:, f, :].bitcast(F32), ALU.subtract
                                    ).then_inc(L("ckv_low"), 1)
                dve.wait_ge(*L("bg_ready", 1))
                V.tensor_copy(BG, PS[5][:, 0:32]).then_inc(L("bg_taken"), 1)
                dve.wait_ge(*L("bg_taken", 1))
                B, G = BG[:, 0:16], BG[:, 16:32]
                V.memset(MPREV[:, 0:4], M_INIT)
                then(V.tensor_tensor(U.rearrange("p (n c) -> p n c", n=NT), i_pre,
                                     B.rearrange("p (n c) -> p n c", n=NT), ALU.subtract))
                for n in range(NT):
                    h4 = slice(4 * n, 4 * n + 4)
                    if n:
                        dve.wait_ge(*L("ub_ready", n))
                    V.tensor_tensor(heads(DG, 4), over(IDENT[:, :], 4), bcast(U[:, h4], 4, P), ALU.mult
                                    ).then_inc(L("diag_ready"), 1)
                    ub = heads(PS[6 + n % 2][:, :], 4)
                    dve.wait_ge(*L("ub_ready", n + 1))
                    then(V.tensor_reduce(MAXU[:, h4], ub, AX.X, ALU.max))
                    if n:
                        dve.wait_ge(*L("swt_ready", n))
                    V.tensor_tensor(heads(DM, 4), ub, over(CAUSAL[:, 3 * P:], 4), ALU.add
                                    ).then_inc(L("ub_taken"), 1)
                    dve.wait_ge(*L("ub_taken", n + 1))
                    V.tensor_reduce(RMAX[:, h4], heads(DM, 4), AX.X, ALU.max)
                    V.tensor_tensor(MLOC, G[:, h4], MAXU[:, h4], ALU.add)
                    then(V.tensor_tensor(GM, G[:, h4], MPREV[:, h4], ALU.add))
                    arg = ARG[:, 20 * n:20 * n + 20]
                    V.tensor_tensor(MPREV[:, 4 * n + 4:4 * n + 8], GM, MLOC, ALU.max)
                    then(V.tensor_tensor(MX[:, h4], MPREV[:, h4], RMAX[:, h4], ALU.max))
                    V.tensor_tensor(arg[:, 0:4], U[:, h4], MAXU[:, h4], ALU.subtract)
                    V.tensor_tensor(arg[:, 4:8], MPREV[:, h4], MX[:, h4], ALU.subtract)
                    V.scalar_tensor_tensor(arg[:, 8:12], B[:, h4], -1.0, MX[:, h4], ALU.mult, ALU.subtract)
                    V.tensor_tensor(arg[:, 12:16], GM, MPREV[:, 4 * n + 4:4 * n + 8], ALU.subtract)
                    V.tensor_tensor(arg[:, 16:20], MLOC, MPREV[:, 4 * n + 4:4 * n + 8], ALU.subtract)
                    V.tensor_tensor(heads(DM, 4), heads(DM, 4), bcast(MX[:, h4], 4, P), ALU.subtract
                                    ).then_inc(L("darg_ready"), 1)
                    w_loc, s_inter, floor = arg[:, 0:4], arg[:, 4:8], arg[:, 8:12]
                    s_old, s_loc = arg[:, 12:16], arg[:, 16:20]
                    dve.wait_ge(*L("pex_ready", n + 1))
                    dve.wait_ge(*L("ms_ready", n + 1))
                    V.tensor_tensor(DM, DM, PS[0][:, :], ALU.mult).then_inc(L("sw_ready"), 1)
                    vw, tot, ct = heads(VW, 4), heads(TOT, 4), heads(CT, 4)
                    if n < NT - 1:
                        if n:
                            dve.wait_ge(*L("cl_ready", n))
                        V.tensor_tensor(vw, VEXT[:, n, :, :], bcast(w_loc, 4, 129), ALU.mult
                                        ).then_inc(L("vw_ready"), 1)

                    def pair(b, e):
                        return PS[b][:, 0:258].rearrange("p (h d) -> p h d", h=2)

                    if n:
                        dve.wait_ge(*L("n2_ready", n))
                        for e, b in enumerate((1, 7 - n % 2)):
                            ins = V.tensor_tensor(tot[:, 2 * e:2 * e + 2, :], pair(b, e),
                                                  bcast(s_inter[:, 2 * e:2 * e + 2], 2, 129), ALU.mult)
                        ins.then_inc(L("n2_taken"), 1)
                        dve.wait_ge(*L("n2_taken", n))
                    dve.wait_ge(*L("n1_ready", n + 1))
                    for e, b in enumerate((5, 0)):
                        t_ = tot[:, 2 * e:2 * e + 2, :]
                        if n:
                            ins = V.tensor_tensor(t_, t_, pair(b, e), ALU.add)
                        else:
                            ins = V.tensor_copy(t_, pair(b, e))
                    ins.then_inc(L("tot_ready"), 1)
                    if n < NT - 1:
                        dve.wait_ge(*L("cl_ready", n + 1))
                        if n:
                            V.tensor_tensor(ct, ct, bcast(s_old, 4, 129), ALU.mult)
                            for e, b in enumerate((2, 3)):
                                ins = V.tensor_tensor(vw[:, 2 * e:2 * e + 2, :], pair(b, e),
                                                      bcast(s_loc[:, 2 * e:2 * e + 2], 2, 129), ALU.mult)
                            then(ins)
                            V.tensor_tensor(ct, ct, vw, ALU.add).then_inc(L("state_ready"), 1)
                        else:
                            for e, b in enumerate((2, 3)):
                                ins = V.tensor_tensor(ct[:, 2 * e:2 * e + 2, :], pair(b, e),
                                                      bcast(s_loc[:, 2 * e:2 * e + 2], 2, 129), ALU.mult)
                            ins.then_inc(L("state_ready"), 1)
                    dve.wait_ge(*L("tot_ready", n + 1))
                    den = tot[:, :, 128:129].rearrange("p h o -> p (h o)")
                    then(V.scalar_tensor_tensor(AD[:, 0:4], den, -1.0, den, ALU.mult, ALU.max))
                    then(V.tensor_tensor(AD[:, 0:4], AD[:, 0:4], floor, ALU.max))
                    then(V.reciprocal(AD[:, 4:8], AD[:, 0:4]))
                    then(V.tensor_tensor(heads(HALL[:, n, :], 4), tot[:, :, 0:M_DH],
                                         bcast(AD[:, 4:8], 4, M_DH), ALU.mult))
                squares(lambda n: HALL[:, n, :], 4, "h")
                dve.wait_ge(*L("mo_ready", NT))
                for n in range(NT):
                    h_ = HALL[:, n, :]
                    then(V.tensor_tensor(heads(h_, 4), heads(h_, 4), bcast(RSH[:, 4 * n:4 * n + 4], 4, M_DH),
                                         ALU.mult))
                    then(V.tensor_tensor(h_, h_, row("m_norm_g"), ALU.mult))
                    V.tensor_tensor(h_, h_, MO[:, n, :], ALU.mult).then_inc(L("ya_tm"), 1)

                dve.wait_ge(*L("sk_raw", NT))
                dve.wait_ge(*L("tr_ready", 9))
                norm_and_turn(TA, "sk_g", "sk")
                dve.wait_ge(*L("dq_raw", NT))
                norm_and_turn(TB, "dq_g", "dq")
                M0 = (None, 0, 256, 640)
                for n in range(1, NT):
                    w = (n + 1) * P
                    m = MSK[:, M0[n]:M0[n] + w]
                    for h in range(IDX_HEADS):
                        i = 4 * (n - 1) + h
                        dve.wait_ge(*L("relu_ready", i + 1))
                        r, wi = RELU[:, i % 2, 0:w], WI[:, 4 * n + h:4 * n + h + 1]
                        if h == 0:
                            V.tensor_scalar(m, r, wi, 0.0, ALU.mult, ALU.add).then_inc(L("idx_used"), 1)
                        else:
                            dve.wait_ge(*L("idx_used", i))
                            V.scalar_tensor_tensor(m, r, wi, m, ALU.mult, ALU.add
                                                   ).then_inc(L("idx_used"), 1)
                    dve.wait_ge(*L("idx_used", 4 * n))
                    last = m[:, n * P:w]
                    then(V.scalar_tensor_tensor(last, CAUSAL[:, 3 * P:], CAUSAL_FILL / MASKED, last,
                                                ALU.mult, ALU.add))
                dve.wait_ge(*L("dk_raw", NT))
                norm_and_turn(TA, "dk_g", "dk")

                TOP_ROUNDS = TOPK // 8

                def mark_top(round_):
                    n = 1 + round_ // TOP_ROUNDS
                    m = MSK[:, M0[n]:M0[n] + (n + 1) * P]
                    then(V.max(TOP8, m))
                    then(V.match_replace(m, TOP8, m, TAKEN))
                    if round_ % TOP_ROUNDS == TOP_ROUNDS - 1:
                        then(V.tensor_scalar(m, m, (TAKEN + CAUSAL_FILL) / 2, MASKED, ALU.is_gt, ALU.mult))

                for a in range(2):
                    for q in range(9):
                        if q < 8:
                            n = q // 2
                            w = (n + 1) * P
                            mask = (MSK[:, M0[n]:M0[n] + w] if a and n else
                                    CAUSAL[:, (NT - 1 - n) * P:])
                            i0 = 8 * (n % 2) + 4 * (q % 2)
                            for j in range(4):
                                dve.wait_ge(*L("att_s", 32 * a + 4 * q + j + 1))
                                V.tensor_tensor_reduce(
                                    out=SS[:, q % 2, j, 0:w], in0=PS[j][:, 0:w], in1=mask, scale=0.125,
                                    scalar=-3.0e38, op0=ALU.add, op1=ALU.max,
                                    accum_out=MXS[:, i0 + j:i0 + j + 1]).then_inc(L("att_max"), 1)
                            dve.wait_ge(*L("att_max", 32 * a + 4 * q + 4))
                            V.tensor_scalar(MXS[:, i0:i0 + 4], MXS[:, i0:i0 + 4], -1.0, 0.0, ALU.mult,
                                            ALU.add).then_inc(L("att_neg"), 1)
                            if a == 0:
                                for r in range(6):
                                    mark_top(6 * q + r)
                        if not q:
                            continue
                        p = q - 1
                        n = p // 2
                        w = (n + 1) * P
                        i0 = 8 * (n % 2) + 4 * (p % 2)
                        if a == 0:
                            dve.wait_ge(*L("att_e", 4 * p + 4))
                            then(V.reciprocal(RS_[:, i0:i0 + 4], SUMS[:, i0:i0 + 4]))
                            for j in range(2):
                                V.tensor_scalar(NLR[:, j:j + 1], RS_[:, i0 + 2 * j + 1:i0 + 2 * j + 2],
                                                LAM[:, 4:5], 0.0, ALU.mult, ALU.add)
                                first = SS[:, p % 2, 2 * j, 0:w]
                                then(V.tensor_scalar(first, first, RS_[:, i0 + 2 * j:i0 + 2 * j + 1], 0.0,
                                                     ALU.mult, ALU.add))
                                V.scalar_tensor_tensor(first, SS[:, p % 2, 2 * j + 1, 0:w],
                                                       NLR[:, j:j + 1], first, ALU.mult, ALU.add
                                                       ).then_inc(L("att_p"), 1)
                        if p % 2:
                            dve.wait_ge(*L("att_o", P_BASE[a] + (2 if a == 0 else 4) * (p + 1)))
                            y = PS[6 + n % 2][:, :]
                            if a == 0:
                                V.tensor_copy(TA[:, n, :], y).then_inc(L("att_y"), 1)
                            else:
                                i8 = 8 * (n % 2)
                                then(V.reciprocal(RS_[:, i8:i8 + 8], SUMS[:, i8:i8 + 8]))
                                dve.wait_ge(*L("tr_ready", 29))
                                V.tensor_tensor(heads(TA[:, n, :], 8), heads(y, 8),
                                                bcast(RS_[:, i8:i8 + 8], 8, S_DH), ALU.mult
                                                ).then_inc(L("att_y"), 1)
                    if a == 0:
                        dve.wait_ge(*L("att_y", NT))
                        squares(lambda n: TA[:, n, :], DA_HEADS, "yc")
                        for n in range(NT):
                            t3 = heads(TA[:, n, :], 4)
                            then(V.tensor_tensor(t3, t3, bcast(RSH[:, 4 * n:4 * n + 4], 4, P), ALU.mult))
                            ins = V.tensor_tensor(t3, t3, over(row("d_out_g"), 4), ALU.mult)
                        ins.then_inc(L("y_tm"), 1)

                for i, Y in enumerate((YA, YB, YC)):
                    dve.wait_ge(*L("y_high", i + 1))
                    V.tensor_tensor(YL[:, 4 * i:4 * i + 4, :], Y[:, :, :],
                                    YH[:, 4 * i:4 * i + 4, :].bitcast(F32), ALU.subtract
                                    ).then_inc(L("y_low"), 1)

                def merge(dt):
                    if not isinstance(dt, int):
                        dve.wait_ge(*L("merged_ready", dt))
                    for r in range(3):
                        dve.wait_ge(*L("gate_ready", dt * 3 + (r + 1)))
                        dve.wait_ge(S("chunk_done"), dt * 6 + (seg("gates") + 2 * r + 2))
                        V.tensor_tensor(GACC[:, min(r, 1), :], SG[r], PS[2 * r + 1][:, :], ALU.mult
                                        ).then_inc(L("gate_used"), 1)
                        if r:
                            dve.wait_ge(*L("gate_used", dt * 3 + (r + 1)))
                            then(V.tensor_tensor(GACC[:, 0, :], GACC[:, 0, :], GACC[:, 1, :], ALU.add))
                    at_ = bass.ds(dt, 1)
                    split(MH[:, at_, :].rearrange("p a t -> p (a t)"),
                          ML[:, at_, :].rearrange("p a t -> p (a t)"), GACC[:, 0, :], L("merged_ready"))

                steady(8, merge)
                add_residual(2 * li, (6, 7), seg("wout"), 1)
                norm(2 * li + 1, col(li, "ffn_g"))

                def hidden(i):
                    for t in range(2):
                        dve.wait_ge(*L("silu_ready", i * 2 + (t + 1)))
                        dve.wait_ge(S("chunk_done"), i * 4 + (seg("ffn") + 2 * t + 2))
                        V.tensor_tensor(HT[:, t, :], SILU[:, t, :], PS[2 * t + 1][:, :], ALU.mult
                                        ).then_inc(L("hidden_used"), 1)
                        dve.wait_ge(*L("hidden_used", i * 2 + (t + 1)))
                        at_ = bass.ds(i * 2 + t, 1)
                        split(HH[:, at_, :].rearrange("p a t -> p (a t)"),
                              HL[:, at_, :].rearrange("p a t -> p (a t)"), HT[:, t, :],
                              L("hidden_ready"))

                steady(KF // 2, hidden)
                add_residual(2 * li + 1, (4, 5), seg("down"), 4)

            dve.wait_ge(S("consts"), 16 * 7)
            for li in range(DEPTH):
                layer(li)

            norm(4, col2("even_g"))
            dve.wait_ge(S("even_consts"), 16 * 3)
            V.tensor_tensor(WS[:, :, :], WS[:, :, :], TRI[:, :].unsqueeze(1).to_broadcast([P, 4, P]),
                            ALU.mult).then_inc(S("ws_masked"), 1)
            for g, size in enumerate(POOL_SIZES):
                dve.wait_ge(S("e_a"), 2 * g + 2)
                src, shift = EA[:, :, :], 1
                for level in range(g + 1):
                    dst = ES[:, level % 2, :, :]
                    V.tensor_copy(dst[:, :, 0:shift], src[:, :, 0:shift])
                    then(V.tensor_tensor(dst[:, :, shift:], src[:, :, shift:], src[:, :, 0:T - shift],
                                         ALU.add))
                    src, shift = dst, 2 * shift
                other = ES[:, (g + 1) % 2, :, :]
                V.tensor_tensor(other[:, :, 0:16], src[:, :, 0:16],
                                INV[:, g, :].unsqueeze(1).to_broadcast([P, 2, 16]), ALU.mult)
                then(V.tensor_scalar(other[:, :, 16:], src[:, :, 16:], 1.0 / size, 0.0, ALU.mult, ALU.add))
                then(V.tensor_tensor(src, other, EA[:, :, :], ALU.subtract))
                then(V.tensor_copy(PLH[:, :, :], src))
                V.tensor_tensor(PLL[:, :, :], src, PLH[:, :, :].bitcast(F32), ALU.subtract
                                ).then_inc(S("pooled_ready"), 1)
                dve.wait_ge(S("e_ga"), 2 * g + 2)
                dve.wait_ge(S("chunk_done"), FIRST["epool"] + 7 * g + 7)
                for t in range(2):
                    j = 2 * g + t
                    then(V.scalar_tensor_tensor(ET[:, t, :], PS[t][:, :], col2("pool_scale")[:, j:j + 1],
                                                GA[:, t, :], ALU.mult, ALU.mult))
                    split(EYH[:, j, :], EYL[:, j, :], ET[:, t, :], S("ey_ready"))
            for j in range(8):
                b0, e = 4 * (j % 2), ET[:, j % 2, :]
                dve.wait_ge(S("e_mixed"), j + 1)
                then(V.tensor_tensor(heads(e, 4), heads(PS[b0][:, :], 4),
                                     BS[:, j // 2, :].unsqueeze(1).to_broadcast([P, 4, P]), ALU.add))
                dve.wait_ge(S("chunk_done"), FIRST["eug"] + 2 * j + 1)
                then(V.tensor_tensor(e, e, PS[b0 + 1][:, :], ALU.mult))
                dve.wait_ge(S("e_gb"), j + 1)
                then(V.tensor_tensor(e, e, GA[:, j % 2, :], ALU.mult))
                split(EYH[:, 8 + j, :], EYL[:, 8 + j, :], e, S("ey_ready"))
            add_residual(4, (3, 7), FIRST["eout"], 2)

            norm(5, col2("odd_g"))
            dve.wait_ge(S("odd_consts"), 16 * 2)

            def slots(i):
                for t in range(2):
                    s = i * 2 + t
                    for n in range(NT + 1):
                        if n < NT:
                            at_ = 0
                            for g in range(N_DIL):
                                w = (min(n, 1) + 1 if g == 0 else n + 1) * P
                                d1 = (2, 6, 10)[g] * P
                                dve.wait_ge(S("o_s"), s * 12 + (3 * n + g + 1))
                                V.scalar_tensor_tensor(
                                    OS[:, n % 2, at_:at_ + w], DIST[:, d1 - w:d1],
                                    SLOPE[:, bass.ds(s + 8 * g, 1)], PS[g][:, 0:w], ALU.mult, ALU.add
                                    ).then_inc(S("o_sc"), 1)
                                at_ += w
                            dve.wait_ge(S("o_sc"), s * 12 + (3 * n + 3))
                            then(V.tensor_reduce(OMX[:, n:n + 1], OS[:, n % 2, 0:at_], AX.X, ALU.max))
                            V.tensor_scalar(OMX[:, n:n + 1], OMX[:, n:n + 1], -1.0, 0.0, ALU.mult, ALU.add
                                            ).then_inc(S("o_neg"), 1)
                        if n:
                            m = n - 1
                            dve.wait_ge(S("o_o"), s * 4 + n)
                            then(V.reciprocal(OMX[:, 4 + m:5 + m], OMX[:, 4 + m:5 + m]))
                            V.tensor_scalar(OO[:, m % 2, :], PS[6 + m % 2][:, 0:P], OMX[:, 4 + m:5 + m],
                                            0.0, ALU.mult, ALU.add).then_inc(S("o_on"), 1)
                    dve.wait_ge(S("o_ot"), s * 4 + 4)
                    dve.wait_ge(S("ogc_ready"), s + 1)
                    then(V.tensor_tensor(OT[:, t, :], PS[3][:, :], GC[:, t, :], ALU.mult))
                    at_ = bass.ds(s, 1)
                    split(OYH[:, at_, :].rearrange("p a t -> p (a t)"),
                          OYL[:, at_, :].rearrange("p a t -> p (a t)"), OT[:, t, :], S("oy_ready"))

            steady(4, slots)
            dve.wait_ge(S("oy_ready"), 8)
            then(V.memset(OZ[:, :, 0:2], 0.0))
            at_w = COL2_AT["conv_w"][0]

            def conv(i):
                for t in range(2):
                    z, acc = OZ[:, t, :], OACC[:, t, :]
                    dve.wait_ge(S("od_c"), i * 2 + (t + 1))
                    dve.wait_ge(S("chunk_done"), i * 8 + (FIRST["od"] + 4 * t + 2))
                    V.tensor_tensor(z[:, 2:], ODC[:, t, :], PS[4 * t + 1][:, :], ALU.mult
                                    ).then_inc(S("od_x"), 1)
                    dve.wait_ge(S("od_x"), i * 2 + (t + 1))

                    def weight(tap):
                        return COL2[:, bass.ds(i * 2 + (at_w + 8 * tap + t), 1)]

                    then(V.tensor_scalar(acc, z[:, 0:T], weight(0), 0.0, ALU.mult, ALU.add))
                    for tap in (1, 2):
                        then(V.scalar_tensor_tensor(acc, z[:, tap:tap + T], weight(tap), acc, ALU.mult,
                                                    ALU.add))
                    dve.wait_ge(S("chunk_done"), i * 8 + (FIRST["od"] + 4 * t + 3))
                    V.tensor_tensor(acc, acc, PS[4 * t + 2][:, :], ALU.mult).then_inc(S("od_b"), 1)
                    dve.wait_ge(S("od_b"), i * 2 + (t + 1))
                    dve.wait_ge(S("od_g"), i * 2 + (t + 1))
                    then(V.tensor_tensor(acc, acc, OGD[:, t, :], ALU.mult))
                    at_ = bass.ds(i * 2 + (8 + t), 1)
                    split(OYH[:, at_, :].rearrange("p a t -> p (a t)"),
                          OYL[:, at_, :].rearrange("p a t -> p (a t)"), acc, S("od_ready"))

            steady(4, conv)
            add_residual(5, (0, 4), FIRST["oout"], 2)
            norm(6, col2("final_g"), final=True)


def lay_out(inputs):
    a = {k: np.asarray(v) for k, v in inputs.items()}

    def tiles(w, cols):
        k, n = w.shape
        return w.reshape(k // P, P, n // cols, cols).transpose(2, 1, 0, 3).reshape(n // cols, P, -1)

    def k_pairs(w, per=2):
        k, n = w.shape
        return w.reshape(k // (per * P), per, P, n).transpose(0, 2, 1, 3).reshape(-1, P, per * n)

    seg = {}
    sizes = [1024, 512, 512, 8, 512, 256, 256, 64, 4, 512, 512, 512, 3072]
    for li in range(DEPTH):
        L = f"L{li}"
        cuts = np.split(a["w_in"][li], np.cumsum(sizes)[:-1], axis=1)
        m_qk, m_v, m_o, m_if, s_q, ckv, i_q, i_k, i_w, d_q, d_k, d_v, g_pre = cuts
        seg[L + "conv"] = [tiles(m_qk, P)]
        seg[L + "mv"], seg[L + "mo"] = [k_pairs(m_v)], [k_pairs(m_o)]
        seg[L + "small"] = [k_pairs(np.concatenate([i_k, i_w, m_if], 1), KD)]
        seg[L + "sq"] = [k_pairs(s_q)]
        seg[L + "ckvq"] = [k_pairs(np.concatenate([ckv, i_q], 1))]
        up = a["dsa_w_kv_up"][li]
        seg[L + "kvup"] = [np.concatenate([k_pairs(up[:, :512]), k_pairs(up[:, 512:])])]
        seg[L + "dq"], seg[L + "dk"], seg[L + "dv"] = [k_pairs(d_q)], [k_pairs(d_k)], [k_pairs(d_v)]
        gate = tiles(g_pre, P).reshape(3, 8, P, 1024).transpose(1, 0, 2, 3).reshape(24, P, 1024)
        branch = np.stack([tiles(a["w_branch"][li, r], P) for r in range(3)], 1).reshape(24, P, 512)
        seg[L + "gates"] = [gate, branch]
        seg[L + "wout"] = [tiles(a["w_out"][li], P)]
        gu = a["w_gate_up"][li]
        seg[L + "ffn"] = [tiles(gu[:, :FF], P), tiles(gu[:, FF:], P)]
        down = tiles(a["w_down"][li], P)
        seg[L + "down"] = list(np.split(down, [768, 1536, 2176], axis=2))
    e = a["even_w_in_2"][0]
    e_a, e_ga, e_u, e_v, e_gb = np.split(e, 5, axis=1)
    ta, tg = tiles(e_a, P), tiles(e_ga, P)
    v_chunks = np.stack([k_pairs(e_v[:, :512]), k_pairs(e_v[:, 512:])]).reshape(8, P, 1024)
    pool = a["even_pool_w_2"][0].reshape(4, 2, P, 256).transpose(0, 2, 1, 3).reshape(4, P, 512)
    seg["epool"] = [ta[0::2], ta[1::2], tg[0::2], tg[1::2], v_chunks[0::2], v_chunks[1::2], pool]
    seg["eug"] = [tiles(e_u, P), tiles(e_gb, P)]
    seg["eout"] = list(np.split(tiles(a["even_w_out_2"][0], P), 2, axis=2))
    o = a["odd_w_in_2"][0]
    qkv, g_c, d_b, d_c, d_x, g_d = np.split(o, [9216, 10240, 11264, 12288, 13312], axis=1)
    qkv = qkv.reshape(D, 3, N_DIL, N_SLOT, P)
    qk = [tiles(qkv[:, r, g].reshape(D, N_SLOT * P), P) for r in range(2) for g in range(N_DIL)]
    v = qkv[:, 2].transpose(0, 2, 1, 3).reshape(D, N_SLOT, 384)
    v = np.stack([k_pairs(v[:, s]) for s in range(N_SLOT)])
    seg["oslot"] = qk + [tiles(g_c, P)] + [v[:, q] for q in range(4)]
    seg["od"] = [tiles(w, P) for w in (d_c, d_x, d_b, g_d)]
    seg["oout"] = list(np.split(tiles(a["odd_w_out_2"][0], P), 2, axis=2))

    def col(v):
        return v.reshape(-1, P).T

    cols = [np.concatenate([col(a["norm_mix_g"][li]), col(a["mlstm_conv_w"][li]),
                            col(a["mlstm_conv_b"][li]), col(a["b_gate"][li]), col(a["norm_ffn_g"][li])], 1)
            for li in range(DEPTH)]
    rows = [np.concatenate([a["mlstm_gate_b"][li], a["mlstm_norm_g"][li].ravel(), a["dsa_kv_norm_g"][li],
                            a["dsa_q_norm_g"][li], a["dsa_k_norm_g"][li], a["diff_q_norm_g"][li],
                            a["diff_k_norm_g"][li], a["diff_lambda"][li].ravel(),
                            a["diff_out_norm_g"][li]]) for li in range(DEPTH)]
    col2 = np.concatenate([col(a["even_norm_2"][0]), col(a["even_pool_scale_2"][0]),
                           col(a["odd_norm_2"][0]), col(a["odd_conv_w_2"][0]), col(a["final_norm_2"])], 1)
    inv = (1.0 / (np.float32(10000.0) ** (np.arange(0, S_DH, 2, dtype=np.float32) / np.float32(S_DH)))
           ).astype(np.float32)
    ang = np.arange(T, dtype=np.float32)[:, None] * inv[None, :]
    cos, sin = np.cos(ang), np.sin(ang)
    cos = np.concatenate([cos, cos], 1).reshape(NT, P, S_DH).transpose(1, 0, 2)
    sin = np.concatenate([-sin, sin], 1).reshape(NT, P, S_DH).transpose(1, 0, 2)
    t, s = np.arange(P)[:, None], np.arange(T)[None, :]
    back = 3 * P + t - s
    causal = np.where(back >= 0, 0.0, MASKED)
    dist = [np.where((back >= 0) & (back <= T_) & (back % d == 0), back, FAR)
            for d, T_ in zip(DILATIONS, (P, 4 * P, 16 * P))]
    dist = np.concatenate([dist[0][:, 2 * P:], dist[1], dist[2]], 1)
    slope = -(2.0 ** (-8.0 * (np.arange(24) + 1) / 24)).astype(np.float32)[None]
    counts = np.stack([1.0 / np.minimum(np.arange(16) + 1, w) for w in POOL_SIZES]).reshape(1, 64)
    f = np.float32
    small = {
        "x": a["x"][0].T.reshape(KD, P, T), "col": np.stack(cols, 1), "row": np.stack(rows),
        "cos": cos.astype(f), "sin": sin.astype(f), "causal": causal.astype(f), "col2": col2,
        "tri": np.triu(np.ones((P, P), f)), "ident": np.eye(P, dtype=f),
        "ws": a["even_ws_2"][0].transpose(2, 0, 1), "bs": a["even_bs_2"][0].reshape(1, 512),
        "inv": counts.astype(f), "dist": dist.astype(f), "slope": slope,
    }
    return small, seg


def kernel(**inputs):
    import concourse.bacc as bacc
    from concourse.bass_utils import run_bass_kernel_spmd

    small, seg = lay_out(inputs)
    nc = bacc.Bacc("TRN2", target_bir_lowering=False, num_devices=1)
    arrays, dram, weights = {}, {}, {}

    def give(name, array):
        arrays[name] = np.ascontiguousarray(array)
        return nc.dram_tensor(name, array.shape, F32, kind="ExternalInput").ap()

    for name, array in small.items():
        dram[name] = give(name, array)
    for name, items, widths in SEGMENTS:
        weights[name] = [give(f"w_{name}_{q}", piece) for q, piece in enumerate(seg[name])]
        assert [w.shape[-1] for w in weights[name]] == widths and weights[name][0].shape[0] == items
    out = nc.dram_tensor("out", (KD, P, T), F32, kind="ExternalOutput").ap()
    build(nc, dram, weights, out)
    got = run_bass_kernel_spmd(nc, [arrays], core_ids=[0]).results[0]["out"]
    return np.asarray(got).reshape(D, T).T[None]
```
